# Optimizing a Trainium2 kernel written in Bass

```python
import jax, jax.numpy as jnp
from jax import lax
import numpy as np
import math

D_MODEL = 2048
BATCH = 1
SEQ = 256
DEPTH = 1

N_HEADS = 16
HEAD_DIM = 64
N_KV = 4
HEADS_PER_KV = N_HEADS // N_KV
ATTN_WIDTH = N_HEADS * HEAD_DIM
KV_WIDTH = N_KV * HEAD_DIM
N_NSA_BRANCHES = 3
CMP_BLOCK = 32
CMP_STRIDE = 16
CMP_HIDDEN = 4 * HEAD_DIM
SEL_BLOCK = 64
N_SEL = 16
N_FORCED_LOCAL = 2
WINDOW = 512
Q_CHUNK = 32
FORCE_BONUS = 1e4
NEG_INF = -1e30
ROPE_THETA = 500000.0
ROPE_DIM = HEAD_DIM // 4
HEAD_OUT_WIDTH = D_MODEL // N_HEADS
MAX_POS_OFFSET = 1024
POOL_WINDOWS = (2, 4, 8, 16)
POOL_GROUPS = 4
POOL_WIDTH = 1024
POOL_GROUP_WIDTH = POOL_WIDTH // POOL_GROUPS
POOL_OUT_WIDTH = D_MODEL // POOL_GROUPS
N_MERGE_BRANCHES = 2
IN_SPLITS = (ATTN_WIDTH, KV_WIDTH, KV_WIDTH, KV_WIDTH, KV_WIDTH, KV_WIDTH, KV_WIDTH,
             N_HEADS * N_NSA_BRANCHES, POOL_WIDTH, N_MERGE_BRANCHES * D_MODEL)
IN_WIDTH = ATTN_WIDTH + 6 * KV_WIDTH + N_HEADS * N_NSA_BRANCHES + POOL_WIDTH + N_MERGE_BRANCHES * D_MODEL
N_EXPERT_GROUPS = 4
EXPERTS_PER_GROUP = 4
N_EXPERTS = N_EXPERT_GROUPS * EXPERTS_PER_GROUP
TOP_K_EXPERTS = 2
D_EXPERT = 256
RMS_EPS = 1e-6


def _rms(x, g):
    xf = x.astype(jnp.float32)
    inv = lax.rsqrt(jnp.mean(xf * xf, axis=-1, keepdims=True) + RMS_EPS)
    return (xf * inv * g.astype(jnp.float32)).astype(x.dtype)

def _rope_tables(pos):
    inv_freq = ROPE_THETA ** (-jnp.arange(0, ROPE_DIM, 2, dtype=jnp.float32) / ROPE_DIM)
    ang = pos.astype(jnp.float32)[..., None] * inv_freq
    return jnp.cos(ang)[:, :, None, :], jnp.sin(ang)[:, :, None, :]

def _partial_rope(x, cos, sin):
    half = ROPE_DIM // 2
    x1, x2, rest = x[..., :half], x[..., half:ROPE_DIM], x[..., ROPE_DIM:]
    c, s = cos.astype(x.dtype), sin.astype(x.dtype)
    return jnp.concatenate([x1 * c - x2 * s, x2 * c + x1 * s, rest], axis=-1)

def _masked_softmax(s, mask):
    s = jnp.where(mask, s.astype(jnp.float32), NEG_INF)
    return jax.nn.softmax(s, axis=-1) * mask.astype(jnp.float32)

def _compress(kv, pos_emb, w1, w2):
    B, S = kv.shape[:2]
    n_cmp = (S - CMP_BLOCK) // CMP_STRIDE + 1
    idx = np.arange(n_cmp)[:, None] * CMP_STRIDE + np.arange(CMP_BLOCK)[None, :]
    blocks = kv[:, idx] + pos_emb[None, None, :, None, :]
    flat = blocks.transpose(0, 1, 3, 2, 4).reshape(B, n_cmp, N_KV, CMP_BLOCK * HEAD_DIM)
    return jax.nn.silu(flat @ w1) @ w2

def _nsa_attention(q, kc, vc, ks, vs, kw, vw, gates):
    B, S = q.shape[:2]
    n_cmp = kc.shape[1]
    n_blk = S // SEL_BLOCK
    k_top = min(N_SEL, n_blk)
    n_chunks = S // Q_CHUNK
    scale = HEAD_DIM ** -0.5
    cmp_end = np.arange(n_cmp) * CMP_STRIDE + CMP_BLOCK - 1
    a0 = np.arange(n_cmp)[:, None] * CMP_STRIDE
    b0 = np.arange(n_blk)[None, :] * SEL_BLOCK
    ov = np.clip(np.minimum(a0 + CMP_BLOCK, b0 + SEL_BLOCK) - np.maximum(a0, b0), 0, None)
    overlap = jnp.asarray(ov / CMP_BLOCK, dtype=jnp.float32)

    kc_t, vc_t = kc.transpose(0, 2, 1, 3), vc.transpose(0, 2, 1, 3)
    ks_b = ks.reshape(B, n_blk, SEL_BLOCK, N_KV, HEAD_DIM).transpose(0, 3, 1, 2, 4)
    vs_b = vs.reshape(B, n_blk, SEL_BLOCK, N_KV, HEAD_DIM).transpose(0, 3, 1, 2, 4)
    pad = ((0, 0), (0, 0), (WINDOW, 0), (0, 0))
    kw_p = jnp.pad(kw.transpose(0, 2, 1, 3), pad)
    vw_p = jnp.pad(vw.transpose(0, 2, 1, 3), pad)
    q_ch = q.reshape(B, n_chunks, Q_CHUNK, N_KV, HEADS_PER_KV, HEAD_DIM).transpose(1, 0, 3, 4, 2, 5)
    g_ch = gates.reshape(B, n_chunks, Q_CHUNK, N_KV, HEADS_PER_KV, N_NSA_BRANCHES).transpose(1, 0, 3, 4, 2, 5)
    b_ix = jnp.arange(B)[:, None, None, None]
    g_ix = jnp.arange(N_KV)[None, :, None, None]
    blk = jnp.arange(n_blk)

    def chunk(args):
        c, qc, gc = args
        q0 = c * Q_CHUNK
        t = q0 + jnp.arange(Q_CHUNK)
        s = jnp.einsum("bgrqd,bgnd->bgrqn", qc, kc_t) * scale
        p_cmp = _masked_softmax(s, cmp_end[None, :] <= t[:, None])
        o_cmp = jnp.einsum("bgrqn,bgnd->bgrqd", p_cmp.astype(vc_t.dtype), vc_t)
        imp = jnp.einsum("bgrqn,nj->bgqj", p_cmp, overlap)
        dist = (t // SEL_BLOCK)[:, None] - blk[None, :]
        valid_blk = dist >= 0
        forced = (blk[None, :] == 0) | (valid_blk & (dist < N_FORCED_LOCAL))
        score = jnp.where(valid_blk, imp + FORCE_BONUS * forced.astype(jnp.float32), NEG_INF)
        _, sel = lax.top_k(score, k_top)
        ks_g = ks_b[b_ix, g_ix, sel].reshape(B, N_KV, Q_CHUNK, k_top * SEL_BLOCK, HEAD_DIM)
        vs_g = vs_b[b_ix, g_ix, sel].reshape(B, N_KV, Q_CHUNK, k_top * SEL_BLOCK, HEAD_DIM)
        kpos = (sel[..., None] * SEL_BLOCK + jnp.arange(SEL_BLOCK)).reshape(B, N_KV, Q_CHUNK, k_top * SEL_BLOCK)
        mask_s = (kpos <= t[:, None])[:, :, None]
        s = jnp.einsum("bgrqd,bgqkd->bgrqk", qc, ks_g) * scale
        p = _masked_softmax(s, mask_s)
        o_slc = jnp.einsum("bgrqk,bgqkd->bgrqd", p.astype(vs_g.dtype), vs_g)
        kw_c = lax.dynamic_slice_in_dim(kw_p, q0, WINDOW + Q_CHUNK, axis=2)
        vw_c = lax.dynamic_slice_in_dim(vw_p, q0, WINDOW + Q_CHUNK, axis=2)
        wpos = q0 - WINDOW + jnp.arange(WINDOW + Q_CHUNK)
        rel = t[:, None] - wpos[None, :]
        mask_w = (wpos[None, :] >= 0) & (rel >= 0) & (rel < WINDOW)
        s = jnp.einsum("bgrqd,bgkd->bgrqk", qc, kw_c) * scale
        p = _masked_softmax(s, mask_w)
        o_swa = jnp.einsum("bgrqk,bgkd->bgrqd", p.astype(vw_c.dtype), vw_c)
        return gc[..., 0:1] * o_cmp + gc[..., 1:2] * o_slc + gc[..., 2:3] * o_swa

    out = lax.map(chunk, (jnp.arange(n_chunks), q_ch, g_ch))
    return out.transpose(1, 0, 4, 2, 3, 5).reshape(B, S, N_HEADS, HEAD_DIM)

def _multiscale_pool(u):
    B, S, _ = u.shape
    ug = u.reshape(B, S, POOL_GROUPS, POOL_GROUP_WIDTH).astype(jnp.float32)
    csum = jnp.pad(jnp.cumsum(ug, axis=1), ((0, 0), (1, 0), (0, 0), (0, 0)))
    t = np.arange(S)
    outs = []
    for gi, w in enumerate(POOL_WINDOWS):
        lo = np.maximum(t + 1 - w, 0)
        cnt = jnp.asarray((t + 1 - lo).astype(np.float32))
        mean = (csum[:, t + 1, gi] - csum[:, lo, gi]) / cnt[None, :, None]
        outs.append(mean - ug[:, :, gi])
    return jnp.stack(outs, axis=2).astype(u.dtype)

def _mixer_sublayer(x, positions, attn_norm_g, w_in, q_norm_g, k_norm_cmp_g, k_norm_slc_g,
                    k_norm_swa_g, cmp_pos_emb_k, cmp_w1_k, cmp_w2_k, cmp_pos_emb_v, cmp_w1_v,
                    cmp_w2_v, w_head_out, w_pool, pool_scale, w_out):
    B, S, _ = x.shape
    h = _rms(x, attn_norm_g)
    proj = h @ w_in
    splits = np.cumsum(IN_SPLITS)[:-1].tolist()
    (q, k_cmp, v_cmp, k_slc, v_slc, k_swa, v_swa, branch_logits, pool_in,
     merge_logits) = jnp.split(proj, splits, axis=-1)
    q = q.reshape(B, S, N_HEADS, HEAD_DIM)
    kv_shape = (B, S, N_KV, HEAD_DIM)
    k_cmp, v_cmp, k_slc, v_slc, k_swa, v_swa = [a.reshape(kv_shape) for a in (k_cmp, v_cmp, k_slc, v_slc, k_swa, v_swa)]
    cos_t, sin_t = _rope_tables(positions)
    q = _partial_rope(_rms(q, q_norm_g), cos_t, sin_t)
    k_slc = _partial_rope(_rms(k_slc, k_norm_slc_g), cos_t, sin_t)
    k_swa = _partial_rope(_rms(k_swa, k_norm_swa_g), cos_t, sin_t)
    n_cmp = (S - CMP_BLOCK) // CMP_STRIDE + 1
    cmp_end = np.arange(n_cmp) * CMP_STRIDE + CMP_BLOCK - 1
    cos_c, sin_c = _rope_tables(positions[:, cmp_end])
    kc = _partial_rope(_rms(_compress(k_cmp, cmp_pos_emb_k, cmp_w1_k, cmp_w2_k), k_norm_cmp_g), cos_c, sin_c)
    vc = _compress(v_cmp, cmp_pos_emb_v, cmp_w1_v, cmp_w2_v)
    gates = jax.nn.sigmoid(branch_logits.reshape(B, S, N_HEADS, N_NSA_BRANCHES))
    o = _nsa_attention(q, kc, vc, k_slc, v_slc, k_swa, v_swa, gates)
    attn_branch = jnp.einsum("bshd,hde->bshe", o, w_head_out).reshape(B, S, D_MODEL)
    pooled = _multiscale_pool(pool_in)
    pool_branch = jnp.einsum("bsgc,gce->bsge", pooled, w_pool).reshape(B, S, D_MODEL) * pool_scale
    merge = jax.nn.sigmoid(merge_logits.reshape(B, S, N_MERGE_BRANCHES, D_MODEL))
    y = merge[:, :, 0] * attn_branch + merge[:, :, 1] * pool_branch
    return x + y @ w_out

def _moe_sublayer(x, ffn_norm_g, w_router_group, b_router_group, w_router_expert,
                  b_router_expert, w_expert_gate, w_expert_up, w_expert_down):
    B, S, D = x.shape
    ht = _rms(x, ffn_norm_g).reshape(B * S, D)
    T = ht.shape[0]
    g_prob = jax.nn.softmax((ht @ w_router_group).astype(jnp.float32) + b_router_group, axis=-1)
    p_group, g_sel = lax.top_k(g_prob, 1)
    e_logit = ((ht @ w_router_expert).astype(jnp.float32) + b_router_expert).reshape(T, N_EXPERT_GROUPS, EXPERTS_PER_GROUP)
    e_logit = e_logit[jnp.arange(T), g_sel[:, 0]]
    top_val, top_idx = lax.top_k(e_logit, TOP_K_EXPERTS)
    w_top = jax.nn.softmax(top_val, axis=-1) * p_group
    expert_id = g_sel * EXPERTS_PER_GROUP + top_idx
    combine = jnp.sum(jax.nn.one_hot(expert_id, N_EXPERTS, dtype=jnp.float32) * w_top[..., None], axis=1)
    combine = combine.astype(ht.dtype)
    y = jnp.zeros_like(ht)
    for e in range(N_EXPERTS):
        hid = jax.nn.silu(ht @ w_expert_gate[e]) * (ht @ w_expert_up[e])
        y = y + combine[:, e:e + 1] * (hid @ w_expert_down[e])
    return x + y.reshape(B, S, D)

def first_inputs(seed: int = 0) -> dict:
    key = jax.random.key(seed)
    ks = jax.random.split(key, 26)
    f32 = jnp.float32
    L = DEPTH

    def nrm(k, shape, fan_in):
        return jax.random.normal(k, shape, f32) * (fan_in ** -0.5)

    def gain(k, shape):
        return 1.0 + 0.05 * jax.random.normal(k, shape, f32)

    x = jax.random.normal(ks[0], (BATCH, SEQ, D_MODEL), f32)
    positions = (jax.random.randint(ks[1], (BATCH, 1), 0, MAX_POS_OFFSET, dtype=jnp.int32)
                 + jnp.arange(SEQ, dtype=jnp.int32)[None, :])
    return {
        "x": x,
        "positions": positions,
        "attn_norm_g": gain(ks[2], (L, D_MODEL)),
        "w_in": nrm(ks[3], (L, D_MODEL, IN_WIDTH), D_MODEL),
        "q_norm_g": gain(ks[4], (L, HEAD_DIM)),
        "k_norm_cmp_g": gain(ks[5], (L, HEAD_DIM)),
        "k_norm_slc_g": gain(ks[6], (L, HEAD_DIM)),
        "k_norm_swa_g": gain(ks[7], (L, HEAD_DIM)),
        "cmp_pos_emb_k": 0.02 * jax.random.normal(ks[8], (L, CMP_BLOCK, HEAD_DIM), f32),
        "cmp_w1_k": nrm(ks[9], (L, CMP_BLOCK * HEAD_DIM, CMP_HIDDEN), CMP_BLOCK * HEAD_DIM),
        "cmp_w2_k": nrm(ks[10], (L, CMP_HIDDEN, HEAD_DIM), CMP_HIDDEN),
        "cmp_pos_emb_v": 0.02 * jax.random.normal(ks[11], (L, CMP_BLOCK, HEAD_DIM), f32),
        "cmp_w1_v": nrm(ks[12], (L, CMP_BLOCK * HEAD_DIM, CMP_HIDDEN), CMP_BLOCK * HEAD_DIM),
        "cmp_w2_v": nrm(ks[13], (L, CMP_HIDDEN, HEAD_DIM), CMP_HIDDEN),
        "w_head_out": nrm(ks[14], (L, N_HEADS, HEAD_DIM, HEAD_OUT_WIDTH), HEAD_DIM),
        "w_pool": nrm(ks[15], (L, POOL_GROUPS, POOL_GROUP_WIDTH, POOL_OUT_WIDTH), POOL_GROUP_WIDTH),
        "pool_scale": gain(ks[16], (L, D_MODEL)),
        "w_out": nrm(ks[17], (L, D_MODEL, D_MODEL), D_MODEL),
        "ffn_norm_g": gain(ks[18], (L, D_MODEL)),
        "w_router_group": nrm(ks[19], (L, D_MODEL, N_EXPERT_GROUPS), D_MODEL),
        "b_router_group": 0.01 * jax.random.normal(ks[20], (L, N_EXPERT_GROUPS), f32),
        "w_router_expert": nrm(ks[21], (L, D_MODEL, N_EXPERTS), D_MODEL),
        "b_router_expert": 0.01 * jax.random.normal(ks[22], (L, N_EXPERTS), f32),
        "w_expert_gate": nrm(ks[23], (L, N_EXPERTS, D_MODEL, D_EXPERT), D_MODEL),
        "w_expert_up": nrm(ks[24], (L, N_EXPERTS, D_MODEL, D_EXPERT), D_MODEL),
        "w_expert_down": nrm(ks[25], (L, N_EXPERTS, D_EXPERT, D_MODEL), D_EXPERT),
    }

def first_block(x, positions, attn_norm_g, w_in, q_norm_g, k_norm_cmp_g, k_norm_slc_g,
              k_norm_swa_g, cmp_pos_emb_k, cmp_w1_k, cmp_w2_k, cmp_pos_emb_v, cmp_w1_v,
              cmp_w2_v, w_head_out, w_pool, pool_scale, w_out, ffn_norm_g, w_router_group,
              b_router_group, w_router_expert, b_router_expert, w_expert_gate, w_expert_up,
              w_expert_down):
    for layer in range(DEPTH):
        x = _mixer_sublayer(x, positions, attn_norm_g[layer], w_in[layer], q_norm_g[layer],
                            k_norm_cmp_g[layer], k_norm_slc_g[layer], k_norm_swa_g[layer],
                            cmp_pos_emb_k[layer], cmp_w1_k[layer], cmp_w2_k[layer],
                            cmp_pos_emb_v[layer], cmp_w1_v[layer], cmp_w2_v[layer],
                            w_head_out[layer], w_pool[layer], pool_scale[layer], w_out[layer])
        x = _moe_sublayer(x, ffn_norm_g[layer], w_router_group[layer], b_router_group[layer],
                          w_router_expert[layer], b_router_expert[layer], w_expert_gate[layer],
                          w_expert_up[layer], w_expert_down[layer])
    return x


DEPTH_2 = 2

N_META = 16
N_A_LAYERS = DEPTH_2 // 2
N_B_LAYERS = DEPTH_2 - N_A_LAYERS
D_RNN = 5 * D_MODEL // 4
N_GATE_BLOCKS = 16
GATE_BLOCK = D_RNN // N_GATE_BLOCKS
CONV_WIDTH = 4
LRU_C = 8.0
HEAD_DIM_2 = 128
N_DIFF_HEADS = D_MODEL // (2 * HEAD_DIM_2)
QK_WIDTH = 2 * N_DIFF_HEADS * HEAD_DIM_2
V_WIDTH = N_DIFF_HEADS * 2 * HEAD_DIM_2
D_FF = 4 * D_MODEL
ROPE_THETA_2 = 10000.0
Q_BLOCK = 128
NORM_EPS = 1e-6
SUBLN_EPS = 1e-5


def rmsnorm(x, g, eps=NORM_EPS):
    xf = x.astype(jnp.float32)
    xf = xf * lax.rsqrt(jnp.mean(xf * xf, axis=-1, keepdims=True) + eps)
    return (xf * g.astype(jnp.float32)).astype(x.dtype)

def rope_tables(length):
    inv = 1.0 / (ROPE_THETA_2 ** (jnp.arange(0, HEAD_DIM_2, 2, dtype=jnp.float32) / HEAD_DIM_2))
    ang = jnp.arange(length, dtype=jnp.float32)[:, None] * inv[None, :]
    return jnp.cos(ang), jnp.sin(ang)

def apply_rope(x, cos, sin):
    c = cos[None, :, None, None, :].astype(x.dtype)
    s = sin[None, :, None, None, :].astype(x.dtype)
    half = HEAD_DIM_2 // 2
    x1, x2 = x[..., :half], x[..., half:]
    return jnp.concatenate([x1 * c - x2 * s, x2 * c + x1 * s], axis=-1)

def causal_depthwise_conv(x, w, b):
    y = lax.conv_general_dilated(
        x, w[:, None, :].astype(x.dtype), window_strides=(1,),
        padding=[(CONV_WIDTH - 1, 0)], dimension_numbers=('NWC', 'WIO', 'NWC'),
        feature_group_count=x.shape[-1])
    return y + b.astype(x.dtype)

def _linear_combine(left, right):
    a_l, b_l = left
    a_r, b_r = right
    return a_l * a_r, a_r * b_l + b_r

def rglru_block(u, w_in, conv_w, conv_b, w_r, b_r, w_i, b_i, lam, w_out):
    B, L, _ = u.shape
    proj = u @ w_in
    gate = jax.nn.gelu(proj[..., :D_RNN])
    xr = causal_depthwise_conv(proj[..., D_RNN:], conv_w, conv_b)
    xb = xr.reshape(B, L, N_GATE_BLOCKS, GATE_BLOCK)
    r = jax.nn.sigmoid(jnp.einsum('blnc,ncd->blnd', xb, w_r).reshape(B, L, D_RNN).astype(jnp.float32)
                       + b_r.astype(jnp.float32))
    i = jax.nn.sigmoid(jnp.einsum('blnc,ncd->blnd', xb, w_i).reshape(B, L, D_RNN).astype(jnp.float32)
                       + b_i.astype(jnp.float32))
    log_a = -LRU_C * r * jax.nn.softplus(-lam.astype(jnp.float32))
    a = jnp.exp(log_a)
    bvals = jnp.sqrt(-jnp.expm1(2.0 * log_a)) * (i * xr.astype(jnp.float32))
    _, hs = lax.associative_scan(_linear_combine, (a, bvals), axis=1)
    y = hs.astype(u.dtype) * gate
    return y @ w_out

def squared_relu_mlp(u, w1, w2):
    return jnp.square(jax.nn.relu(u @ w1)) @ w2

def shared_kv(h, g, w_kv, cos, sin):
    B, L, _ = h.shape
    kv = rmsnorm(h, g) @ w_kv
    k = apply_rope(kv[..., :QK_WIDTH].reshape(B, L, N_DIFF_HEADS, 2, HEAD_DIM_2), cos, sin)
    v = kv[..., QK_WIDTH:].reshape(B, L, N_DIFF_HEADS, 2 * HEAD_DIM_2)
    return k, v

def causal_diff_attention(q, k, v, lam):
    L = q.shape[1]
    scale = 1.0 / math.sqrt(HEAD_DIM_2)
    bounds = [0] + list(range(N_META, L, Q_BLOCK)) + [L]
    outs = []
    for s, e in zip(bounds[:-1], bounds[1:]):
        scores = jnp.einsum('bqhcd,bkhcd->bhcqk', q[:, s:e], k[:, :e],
                            preferred_element_type=jnp.float32) * scale
        mask = jnp.arange(e)[None, :] <= (s + jnp.arange(e - s))[:, None]
        p = jax.nn.softmax(jnp.where(mask, scores, -jnp.inf), axis=-1)
        attn = p[:, :, 0] - lam * p[:, :, 1]
        outs.append(jnp.einsum('bhqk,bkhe->bqhe', attn.astype(v.dtype), v[:, :e]))
    return jnp.concatenate(outs, axis=1)

def diff_attention_layer(u, k, v, w_q, lam_vecs, subln_g, w_o, cos, sin, lambda_init):
    B, L, _ = u.shape
    q = apply_rope((u @ w_q).reshape(B, L, N_DIFF_HEADS, 2, HEAD_DIM_2), cos, sin)
    lv = lam_vecs.astype(jnp.float32)
    lam = jnp.exp(jnp.sum(lv[0] * lv[1])) - jnp.exp(jnp.sum(lv[2] * lv[3])) + lambda_init
    o = causal_diff_attention(q, k, v, lam)
    o = rmsnorm(o, subln_g, SUBLN_EPS) * (1.0 - lambda_init)
    return o.reshape(B, L, V_WIDTH) @ w_o

def second_inputs(seed: int = 0) -> dict:
    key = jax.random.key(seed)
    ks = jax.random.split(key, 24)
    f32 = jnp.float32

    def nrm(k, shape, fan_in):
        return jax.random.normal(k, shape, f32) * (fan_in ** -0.5)

    def gain(k, shape):
        return 1.0 + 0.05 * jax.random.normal(k, shape, f32)

    u = jax.random.uniform(ks[10], (N_A_LAYERS, D_RNN), f32, minval=0.9, maxval=0.999)
    a0 = u ** (1.0 / LRU_C)
    a_lambda = jnp.log(a0) - jnp.log1p(-a0)
    return {
        "x": jax.random.normal(ks[0], (BATCH, SEQ, D_MODEL), f32),
        "meta_tokens": jax.random.normal(ks[1], (N_META, D_MODEL), f32),
        "a_norm_g": gain(ks[2], (N_A_LAYERS, D_MODEL)),
        "a_w_in": nrm(ks[3], (N_A_LAYERS, D_MODEL, 2 * D_RNN), D_MODEL),
        "a_conv_w": nrm(ks[4], (N_A_LAYERS, CONV_WIDTH, D_RNN), CONV_WIDTH),
        "a_conv_b": 0.02 * jax.random.normal(ks[5], (N_A_LAYERS, D_RNN), f32),
        "a_w_r": nrm(ks[6], (N_A_LAYERS, N_GATE_BLOCKS, GATE_BLOCK, GATE_BLOCK), GATE_BLOCK),
        "a_b_r": 0.02 * jax.random.normal(ks[7], (N_A_LAYERS, D_RNN), f32),
        "a_w_i": nrm(ks[8], (N_A_LAYERS, N_GATE_BLOCKS, GATE_BLOCK, GATE_BLOCK), GATE_BLOCK),
        "a_b_i": 0.02 * jax.random.normal(ks[9], (N_A_LAYERS, D_RNN), f32),
        "a_lambda": a_lambda,
        "a_w_out": nrm(ks[11], (N_A_LAYERS, D_RNN, D_MODEL), D_RNN),
        "kv_norm_g": gain(ks[12], (D_MODEL,)),
        "w_kv": nrm(ks[13], (D_MODEL, QK_WIDTH + V_WIDTH), D_MODEL),
        "b_norm_g": gain(ks[14], (N_B_LAYERS, D_MODEL)),
        "b_w_q": nrm(ks[15], (N_B_LAYERS, D_MODEL, QK_WIDTH), D_MODEL),
        "b_lambda": 0.1 * jax.random.normal(ks[16], (N_B_LAYERS, 4, HEAD_DIM_2), f32),
        "b_subln_g": gain(ks[17], (N_B_LAYERS, 2 * HEAD_DIM_2)),
        "b_w_o": nrm(ks[18], (N_B_LAYERS, V_WIDTH, D_MODEL), V_WIDTH),
        "mlp_norm_g": gain(ks[19], (DEPTH_2, D_MODEL)),
        "mlp_w1": nrm(ks[20], (DEPTH_2, D_MODEL, D_FF), D_MODEL),
        "mlp_w2": nrm(ks[21], (DEPTH_2, D_FF, D_MODEL), D_FF),
        "final_norm_g": gain(ks[22], (D_MODEL,)),
    }

def second_block(x, meta_tokens, a_norm_g, a_w_in, a_conv_w, a_conv_b, a_w_r, a_b_r, a_w_i, a_b_i,
              a_lambda, a_w_out, kv_norm_g, w_kv, b_norm_g, b_w_q, b_lambda, b_subln_g, b_w_o,
              mlp_norm_g, mlp_w1, mlp_w2, final_norm_g):
    B = x.shape[0]
    meta = jnp.broadcast_to(meta_tokens[None].astype(x.dtype), (B, N_META, D_MODEL))
    h = jnp.concatenate([meta, x], axis=1)
    cos, sin = rope_tables(h.shape[1])
    k_sh, v_sh = None, None
    for layer in range(DEPTH_2):
        if layer < N_A_LAYERS:
            j = layer
            h = h + rglru_block(rmsnorm(h, a_norm_g[j]), a_w_in[j], a_conv_w[j], a_conv_b[j],
                                a_w_r[j], a_b_r[j], a_w_i[j], a_b_i[j], a_lambda[j], a_w_out[j])
        else:
            j = layer - N_A_LAYERS
            if j == 0:
                k_sh, v_sh = shared_kv(h, kv_norm_g, w_kv, cos, sin)
            lambda_init = 0.8 - 0.6 * math.exp(-0.3 * layer)
            h = h + diff_attention_layer(rmsnorm(h, b_norm_g[j]), k_sh, v_sh, b_w_q[j], b_lambda[j],
                                         b_subln_g[j], b_w_o[j], cos, sin, lambda_init)
        h = h + squared_relu_mlp(rmsnorm(h, mlp_norm_g[layer]), mlp_w1[layer], mlp_w2[layer])
    h = rmsnorm(h, final_norm_g)
    return h[:, N_META:]


def setup_inputs(seed=0):
    out = dict(first_inputs(seed))
    for name, value in second_inputs(seed + 1).items():
        if name != "x":
            out[name + "_2"] = value
    return out


def reference(
    x, positions, attn_norm_g, w_in, q_norm_g, k_norm_cmp_g, k_norm_slc_g, k_norm_swa_g,
    cmp_pos_emb_k, cmp_w1_k, cmp_w2_k, cmp_pos_emb_v, cmp_w1_v, cmp_w2_v, w_head_out, w_pool,
    pool_scale, w_out, ffn_norm_g, w_router_group, b_router_group, w_router_expert,
    b_router_expert, w_expert_gate, w_expert_up, w_expert_down, meta_tokens_2, a_norm_g_2,
    a_w_in_2, a_conv_w_2, a_conv_b_2, a_w_r_2, a_b_r_2, a_w_i_2, a_b_i_2, a_lambda_2, a_w_out_2,
    kv_norm_g_2, w_kv_2, b_norm_g_2, b_w_q_2, b_lambda_2, b_subln_g_2, b_w_o_2, mlp_norm_g_2,
    mlp_w1_2, mlp_w2_2, final_norm_g_2,
):
    x = first_block(
        x, positions, attn_norm_g, w_in, q_norm_g, k_norm_cmp_g, k_norm_slc_g, k_norm_swa_g,
        cmp_pos_emb_k, cmp_w1_k, cmp_w2_k, cmp_pos_emb_v, cmp_w1_v, cmp_w2_v, w_head_out,
        w_pool, pool_scale, w_out, ffn_norm_g, w_router_group, b_router_group, w_router_expert,
        b_router_expert, w_expert_gate, w_expert_up, w_expert_down,
    )
    return second_block(
        x, meta_tokens_2, a_norm_g_2, a_w_in_2, a_conv_w_2, a_conv_b_2, a_w_r_2, a_b_r_2,
        a_w_i_2, a_b_i_2, a_lambda_2, a_w_out_2, kv_norm_g_2, w_kv_2, b_norm_g_2, b_w_q_2,
        b_lambda_2, b_subln_g_2, b_w_o_2, mlp_norm_g_2, mlp_w1_2, mlp_w2_2, final_norm_g_2,
    )


_drawn_inputs = setup_inputs


def setup_inputs(seed=0):
    import zlib

    import numpy as np

    out = dict(_drawn_inputs(seed))
    spreads = {}
    factors = {'q_norm_g': 4.662,
     'k_norm_cmp_g': 5.221,
     'k_norm_slc_g': 3.815,
     'k_norm_swa_g': 5.253,
     'cmp_pos_emb_k': 8.0,
     'cmp_pos_emb_v': 4.656,
     'b_router_group': 3.125,
     'a_b_r_2': 8.0,
     'a_b_i_2': 8.0,
     'b_norm_g_2': 4.221,
     'b_subln_g_2': 3.05,
     'b_router_expert': 8.0}
    for name, (base, spread) in spreads.items():
        noise = np.random.default_rng([zlib.crc32(name.encode()), seed]).standard_normal(out[name].shape)
        drawn = base * np.exp(spread * noise) if base else spread * noise
        out[name] = __import__('jax').numpy.asarray(drawn.astype(out[name].dtype))
    for name, factor in factors.items():
        out[name] = (out[name] * factor).astype(out[name].dtype)
    return out
```

```python
from contextlib import ExitStack

import numpy as np

import concourse.bass as bass
from concourse import mybir

F32 = mybir.dt.float32
F32R = mybir.dt.float32r
BF16 = mybir.dt.bfloat16
I32 = mybir.dt.int32
ALU = mybir.AluOpType
ACT = mybir.ActivationFunctionType
AX = mybir.AxisListType
ds = bass.ds

P = 128
D = 2048
KT = D // P
S = 256
META = 16
TB = S + META
ALL, QT = slice(0, TB), slice(0, S)
TOK = slice(META, TB)
HEADS, HD, NKV = 16, 64, 4
HPK = HEADS // NKV
KVW = NKV * HD
NB = 3
CMP_BLOCK, CMP_STRIDE = 32, 16
NCMP = (S - CMP_BLOCK) // CMP_STRIDE + 1
CMP_HID = 4 * HD
ATTN_W = HEADS * HD
GATE_COL = ATTN_W + 6 * KVW
POOL_COL = GATE_COL + HEADS * NB
POOL_W = 1024
POOL_ORDER = (3, 2, 1, 0)
MERGE_COL = POOL_COL + POOL_W
NEXP, NGRP, EPG = 16, 4, 4
DEXP = 256
D_RNN = 5 * D // 4
RT = D_RNN // P
RBLK = D_RNN // 16
SUP = 5
CONV = 4
D_FF = 4 * D
CHUNK = D
DH = 8
THETA, ROPE = 500000.0, HD // 4
THETA2, HD2 = 10000.0, 128
EPS, SUB_EPS = 1e-6, 1e-5
LAMBDA_INIT = float(0.8 - 0.6 * np.exp(-0.3))
NEG = -1e30
ROUND = float(1.5 * 2 ** 23)
TWO_PI = (6.28125, float(np.float32(2 * np.pi - 6.28125)), float(2 * np.pi - 6.28125 - np.float32(2 * np.pi - 6.28125)))
PI_IN = 3.1415925
SLOTS = 4
UW = 2048
TILES2 = [(0, META), (META, P), (META + P, P)]
FIRST_BYTE = 16512

STREAM = [("qkv", 20, 10), ("pool", 8, 4), ("wpool", 2, 8), ("merge", 32, 16), ("wout", 16, 8),
          ("experts", 64, 32), ("down", 32, 8), ("a_in", 40, 20), ("a_out", 20, 8),
          ("mlp0", 128, 64), ("v", 16, 8), ("k", 16, 8), ("q", 16, 8), ("o", 16, 8), ("mlp1", 128, 64)]
U0, B0 = {}, {}
_u = _b = 0
for _n, _c, _p in STREAM:
    U0[_n], B0[_n] = _u, _b
    _u, _b = _u + _c, _b + _p
NUNITS = _u

BC = [RBLK * (P * a // RBLK) // P * P for a in range(SUP)]
BWID = [-(-RBLK * (-(-P * (a + 1) // RBLK)) // P) * P - BC[a] for a in range(SUP)]
BOFF = [sum(BWID[:a]) for a in range(SUP)]
BAND_W = sum(BWID)
BPIECES = []
for _a in range(SUP):
    for _m in range(4):
        _r0, _r1 = max(P * _a, RBLK * _m), min(P * _a + P, RBLK * _m + RBLK)
        if _r0 < _r1:
            BPIECES.append((_a, _m, _r0, _r1))


def const_parts():
    k, m = np.arange(P)[:, None], np.arange(P)[None, :]
    same = (k // HD) == (m // HD)
    rot = np.where(same & (m % HD < ROPE // 2) & (k == m + ROPE // 2), -1.0, 0.0) \
        + np.where(same & (m % HD >= ROPE // 2) & (m % HD < ROPE) & (k == m - ROPE // 2), 1.0, 0.0)
    d = np.arange(P) % HD
    freq = np.float32(THETA) ** (-(2 * (d % (ROPE // 2))).astype(np.float32) / np.float32(ROPE))
    t = np.arange(P)[:, None] + P * np.arange(2)[None, :]
    return [
        ("ident", np.eye(P)), ("hones", same), ("rot", rot),
        ("dup0", k == m % HD), ("dup1", k == HD + m % HD),
        ("freq", np.where(d < ROPE, freq, 0.0)[:, None]),
        ("rcnt", np.tile(1.0 / np.arange(1, 17), (P, 1))),
        ("seen", t >= CMP_BLOCK - 1), ("order", np.tile([4, 3, 2, 1], (P, 2))),
    ]


def mask_parts():
    q, k = np.arange(P)[:, None], np.arange(P)[None, :]
    t = (np.arange(P)[:, None, None] + P * np.arange(2)[None, :, None])
    end = np.arange(16)[None, None, :] * CMP_STRIDE + CMP_BLOCK - 1
    return [("ident16", np.eye(P)), ("causal", np.where(k <= q, 0.0, NEG)),
            ("cmpmask", np.where(end <= t, 0.0, NEG).reshape(P, 32))]


def rope2_parts():
    inv = 1.0 / np.float32(THETA2) ** (np.arange(0, HD2, 2, dtype=np.float32) / np.float32(HD2))
    ang = np.arange(TB, dtype=np.float32)[None, :] * inv[:, None].astype(np.float32)
    c, s = np.cos(ang), np.sin(ang)
    return [("cos2", np.concatenate([c, c])), ("sin2", np.concatenate([s, -s]))]


CONST_W = sum(a.shape[1] for _, a in const_parts())
PARAM = {}
_at = CONST_W
for _n, _w in [("g_attn", KT), ("g_ffn", KT), ("g_a", KT), ("g_mlp0", KT), ("g_kv", KT), ("g_b", KT),
               ("g_mlp1", KT), ("g_final", KT), ("pool_scale", KT), ("conv_w", CONV * RT), ("conv_b", RT),
               ("b_r", RT), ("b_i", RT), ("lam", RT), ("g_q", 1), ("g_kc", 1), ("g_ks", 1), ("g_kw", 1),
               ("g_sub", 2), ("pos_k", 16), ("pos_v", 16), ("w2k", 2 * P), ("w2v", 2 * HD),
               ("router", KT * 20), ("router_b", 20)]:
    PARAM[_n] = (_at, _w)
    _at += _w
AUX_W = _at
_at = 0
for _n, _a in const_parts():
    PARAM[_n] = (_at, _a.shape[1])
    _at += _a.shape[1]


class Chain:

    def __init__(self, engine, sem):
        self.e, self.sem, self.n = engine, sem, 0

    def link(self, ins):
        ins.then_inc(self.sem, 1)
        self.n += 1
        self.e.wait_ge(self.sem, self.n)


def mixer_moe_rnn_attention(nc, A, out):
    with ExitStack() as ctx:
        def at(name, shape, word, dt=F32):
            n = int(np.prod(shape[1:])) // (2 if dt == BF16 else 1)
            end = -(-(word + n) // 8) * 8
            assert end <= (nc.sbuf_usable_end - FIRST_BYTE) // 4, (name, end)
            return nc.alloc_sbuf_tensor_at(name, shape, dt, offset=FIRST_BYTE + 4 * word), end

        def sem(name):
            return ctx.enter_context(nc.semaphore(name))

        raw, _ = at("raw", [P, SLOTS, UW], 0)
        low, w = at("low", [P, SLOTS, UW], 0, F32R)
        high, w = at("high", [P, SLOTS, UW], w, F32R)
        hT, w = at("hT", [P, KT, TB], w)
        aux, w = at("aux", [P, AUX_W], w)
        maskb, w = at("maskb", [P, 288], w, BF16)
        ones, w = at("ones", [P, P], w)
        inv, w = at("inv", [P, TB], w)
        sqsum, w = at("sqsum", [P, TB], w)
        zb, w = at("zb", [P, 2, 2, TB], w)
        small, WORK = at("small", [P, 24], w)
        eps, invt, g_q8, sub_eps = small[:, 0:1], small[:, 2:4], small[:, 4:5], small[:, 1:2]

        def par(name, a=0, b=None):
            o, n = PARAM[name]
            return aux[:, o + a:o + (n if b is None else b)]

        def col(name, kt):
            return aux[:, ds(PARAM[name][0] + kt, 1)]

        ident, hones, rot = par("ident"), par("hones"), par("rot")
        dup = [par("dup0"), par("dup1")]
        ident16, causal16, cmp16 = maskb[:, 0:P], maskb[:, P:2 * P], maskb[:, 2 * P:288]

        gh1, w = at("gh1", [P, KT, S], WORK, F32R)
        gl1, w_pb = at("gl1", [P, KT, S], w, F32R)
        pb, w_ym = at("pb", [P, KT, S], w_pb)
        ym, w = at("ym", [P, KT, S], w_ym)
        qT, w_og = at("qT", [P, 8, S], w)
        og, w_wh = at("og", [HD, HPK, S], w_og)
        wh, w_kd = at("wh", [HD, HEADS, P], w_wh)
        kdup, w = at("kdup", [P, 2, NKV, S], w_kd)
        vtok, w_pr = at("vtok", [P, 2, 2, KVW], w)
        probs, w = at("probs", [P, HPK, 528], w_pr)
        pts, w = at("pts", [P, 2, 512], w)
        krope, w = at("krope", [P, 2, S], w)
        kcT, w = at("kcT", [P, NKV, NCMP], w)
        vcT, w = at("vcT", [NCMP, NKV, HD], w)
        gates, w = at("gates", [P, 2, HEADS, NB], w)
        stat, w = at("stat", [P, 64], w)
        xp, w = at("xp", [P, 2, 2, S], w_pr)
        xsq, w = at("xsq", [P, 2, S], w)
        xrt, w = at("xrt", [P, 2, S], w)
        xn, w = at("xn", [P, 2, S], w)
        xs, w = at("xs", [P, 2, S], w)
        ropec, w = at("ropec", [P, S], w_og)
        ropes, w = at("ropes", [P, S], w)
        chid, w = at("chid", [P, 2, 2, NKV * NCMP], w)
        ck, w = at("ck", [P, 4, NKV * NCMP], w)
        assert w <= w_wh
        wgate, _ = at("wgate", [P, KT, HEADS * NB], w_kd)
        angle, _ = at("angle", [P, 6, S], w_ym)
        posi, _ = at("posi", [P, S], w_ym + 6 * S, I32)
        mask32, _ = at("mask32", [P, 288], w_ym + 7 * S)
        xsqr, _ = at("xsqr", [P, KT, S], w_pb)
        cw1 = [at("cw1k", [P, KT, CMP_HID], w_pb)[0], at("cw1v", [P, KT, CMP_HID], w_ym)[0]]
        flat, _ = at("flat", [P, 2, KT, NKV, NCMP], w_wh)
        pw, _ = at("pw", [P, 3, 2, S], w_wh)
        ph, w = at("ph", [P, 8, S], w_ym, F32R)
        pl, w = at("pl", [P, 8, S], w, F32R)
        yh, w = at("yh", [P, KT, S], WORK, F32R)
        yl, w = at("yl", [P, KT, S], w, F32R)
        GA, GB = WORK, WORK + 2 * KT * TB
        HID = GB + 2 * KT * TB
        gh2, w = at("gh2", [P, KT, S], GB, F32R)
        gl2, w = at("gl2", [P, KT, S], w, F32R)
        hidh, _ = at("hidh", [P, 2 * NEXP, S], GA, F32R)
        hidl, w = at("hidl", [P, 2 * NEXP, S], HID, F32R)
        weight, _ = at("weight", [P, 2 * NEXP, S], HID)
        sq, w = at("sq", [P, 2, 2, TB], HID + 2 * KT * TB)
        SQ_END = w
        rg, w = at("rg", [P, KT, 20], w)
        rl, w = at("rl", [P, 2, 20], w)
        r4, w = at("r4", [P, 8, 2, 4], w)
        r44, w = at("r44", [P, 2, NGRP, EPG], w)
        r1, w = at("r1", [P, 8, 2], w)
        comb, w = at("comb", [P, 2, NEXP], w)
        combT, w = at("combT", [NEXP, S], w)

        gh3, w = at("gh3", [P, KT, TB], GB, F32R)
        gl3, w = at("gl3", [P, KT, TB], w, F32R)
        xr, w = at("xr", [P, RT, TB], GA)
        rl3, _ = at("rl3", [P, RT, TB], GA, F32R)
        rr, w = at("rr", [P, 4, TB], w)
        ri, w = at("ri", [P, 4, TB], w)
        ra, w = at("ra", [P, 4, TB], w)
        assert w <= GB
        zp, w = at("zp", [P, 2, 2, TB + CONV], SQ_END)
        rc, w = at("rc", [P, 6, RT], w)
        rh3, w = at("rh3", [P, RT, TB], HID, F32R)
        band, w = at("band", [P, 2, BAND_W], w)
        gh4, w = at("gh4", [P, KT, TB], GB, F32R)
        gl4, w = at("gl4", [P, KT, TB], w, F32R)
        fh, w = at("fh", [P, KT, TB], HID, F32R)
        fl, w = at("fl", [P, KT, TB], w, F32R)
        gh5, w = at("gh5", [P, KT, TB], GA, F32R)
        gl5, w = at("gl5", [P, KT, TB], w, F32R)
        gh6, w = at("gh6", [P, KT, S], GA, F32R)
        gl6, w = at("gl6", [P, KT, S], w, F32R)
        vt2, w = at("vt2", [P, 3, D], GB)
        kT2, w = at("kT2", [P, KT, TB], w)
        oT, w = at("oT", [P, KT, S], w)
        rq, w = at("rq", [P, 2, S], w)
        q2, w = at("q2", [P, 2, 2, S], w)
        swp, w = at("swp", [P, 2, TB], w)
        pr0, w = at("pr0", [P, 2, META + P], w)
        pr1, w = at("pr1", [P, 2, TB], w)
        pt2, w = at("pt2", [P, 5, P], w)
        osq, w = at("osq", [P, 2, S], w)
        ort, w = at("ort", [P, S], w)
        lv, w = at("lv", [P, 4, HD2], SQ_END)
        rk, w = at("rk", [P, 2, TB], w)
        st2, w = at("st2", [P, 24], w)
        gsub, w = at("gsub", [P, 2], w)
        oh, w = at("oh", [P, KT, S], GA, F32R)
        ol, w = at("ol", [P, KT, S], w, F32R)
        gh7, w = at("gh7", [P, KT, S], GB, F32R)
        gl7, w = at("gl7", [P, KT, S], w, F32R)
        result, w = at("result", [P, KT, S], GA)

        acc = ctx.enter_context(nc.psum_tensor("acc", [P, 4, 512], F32))
        psx = ctx.enter_context(nc.psum_tensor("psx", [P, 4, 512], F32))

        raw_in = [sem(f"raw_in{k}") for k in range(SLOTS)]
        hi_ready, lo_ready = sem("hi_ready"), sem("lo_ready")
        unit_done = sem("unit_done")
        acc_free = sem("acc_free")
        aux_in, mask_in, mask_ready, wg_in, pos_in = sem("aux_in"), sem("mask_in"), sem("mask_ready"), sem("wg_in"), sem("pos_in")
        x_in = [sem(f"x_in{j}") for j in range(4)]
        cw_in, wh_in, meta_in = sem("cw_in"), sem("wh_in"), sem("meta_in")
        setup = sem("setup")
        g_hi, g_lo = sem("g_hi"), sem("g_lo")
        sq_ready, sq_used, sq_half = sem("sq_ready"), sem("sq_used"), sem("sq_half")
        stat_mm, stat_rt = sem("stat_mm"), sem("stat_rt")
        chain_act, chain_dve, chain_pool = sem("chain_act"), sem("chain_dve"), sem("chain_pool")
        x_squared = sem("x_squared")
        x_summed = sem("x_summed")
        wg_scaled, gate_mm, gate_z, gates_tanh = sem("wg_scaled"), sem("gate_mm"), sem("gate_z"), sem("gates_tanh")
        angle_ready, table_ready = sem("angle_ready"), sem("table_ready")
        head_sq, head_mm, head_rt, head_n, head_rot, head_s, head_done = (
            sem(n) for n in ("head_sq", "head_mm", "head_rt", "head_n", "head_rot", "head_s", "head_done"))
        raw_aux, aux_taken = sem("raw_aux"), sem("aux_taken")
        chid_mm, chid_act, kc_mm, kc_sq, kc_ss, kc_rt, kc_n, kc_rot, kc_done = (
            sem(n) for n in ("chid_mm", "chid_act", "kc_mm", "kc_sq", "kc_ss", "kc_rt", "kc_n", "kc_rot", "kc_done"))
        pooled, pooled_hi, pooled_lo, wp_half = (
            sem(n) for n in ("pooled", "pooled_hi", "pooled_lo", "wp_half"))
        merge_t = sem("merge_t")
        s_mm, s_max, s_exp, coef, p_scaled, pt_mm, pt_out, o_mm, o_out, ho_mm, ho_out = (
            sem(n) for n in ("s_mm", "s_max", "s_exp", "coef", "p_scaled", "pt_mm", "pt_out", "o_mm", "o_out",
                             "ho_mm", "ho_out"))
        y_done, y_hi, y_lo = sem("y_done"), sem("y_hi"), sem("y_lo")
        rg_ready, rl_mm, comb_exp, comb_z, comb_done, comb_t, comb_c, wt_mm, wt_out = (
            sem(n) for n in ("rg_ready", "rl_mm", "comb_exp", "comb_z", "comb_done", "comb_t", "comb_c", "wt_mm", "wt_out"))
        silu_e, hid_z, hid_hi, hid_lo = (sem(n) for n in ("silu_e", "hid_z", "hid_hi", "hid_lo"))
        band_clear, band_in = sem("band_clear"), sem("band_in")
        xr_done, rg_mm, rg_sig, rg_a, rg_th, rg_e, rg_q, rg_i, rg_x, rg_b = (
            sem(n) for n in ("xr_done", "rg_mm", "rg_sig", "rg_a", "rg_th", "rg_e", "rg_q", "rg_i", "rg_x", "rg_b"))
        lam_z, lam_exp = sem("lam_z"), sem("lam_exp")
        gelu_done, ry_z, ry_hi, ry_lo = (sem(n) for n in ("gelu_done", "ry_z", "ry_hi", "ry_lo"))
        hid_sq = sem("hid_sq")
        rope_in, lv_in, dl_z, dl_exp = (sem(n) for n in ("rope_in", "lv_in", "dl_z", "dl_exp"))
        v_mm, v_out, k_done, q_done = (sem(n) for n in ("v_mm", "v_out", "k_done", "q_done"))
        a_sc, a_max, a_exp, a_attn, a_tr, a_pt, a_pv, a_sq, a_o, a_ss, a_rt, a_od = (
            sem(n) for n in ("a_sc", "a_max", "a_exp", "a_attn", "a_tr", "a_pt", "a_pv", "a_sq", "a_o", "a_ss",
                             "a_rt", "a_od"))
        o_hi, o_lo = sem("o_hi"), sem("o_lo")
        result_ready, stored = sem("result_ready"), sem("stored")

        NT = [3, 5]

        def blocks_of(i):
            return [(b, 256 * b + P * k, k, P) for k in range(i + 1) for b in range(2)] + [(2, 512, 0, NCMP)]

        block = ctx.enter_context(nc.Block())

        @block.sync
        def _(sp):
            def load_x(j):
                sp.dma_start(hT[:, 4 * j:4 * j + 4, TOK], A["x"].rearrange("(kt p) t -> p kt t", p=P)[:, 4 * j:4 * j + 4, :])\
                    .then_inc(x_in[j], 16)

            def pair_units(name, w_dram, c0, npairs, u_off=0, body=2):
                v = w_dram.rearrange("(h kt p) n -> h p kt n", p=P, kt=8)
                nh = v.shape[0]

                def one(u, slot, h, c):
                    sp.wait_ge(unit_done, u - SLOTS + 1)
                    sp.dma_start(raw[:, slot, :].rearrange("p (kt n) -> p kt n", n=256),
                                 v[h, :, :, ds(c, 256)]).then_inc(raw_in[slot], 16)

                with sp.Fori(0, npairs // body) as i:
                    for pr in range(body):
                        for h in range(nh):
                            k = pr * nh + h + U0[name] + u_off
                            one(i * (body * nh) + k, k % SLOTS, h, i * (256 * body) + (c0 + 256 * pr))

            v = A["w_in"].rearrange("(h kt p) n -> h p kt n", p=P, kt=8)
            load_x(0), load_x(1)
            for u in range(SLOTS):
                if u == 1:
                    load_x(2), load_x(3)
                sp.dma_start(raw[:, u, :].rearrange("p (kt n) -> p kt n", n=256),
                             v[u % 2, :, :, 256 * (u // 2):256 * (u // 2) + 256]).then_inc(raw_in[u], 16)
            pair_units("qkv", A["w_in"], 512, 8, 4)
            for j in range(8):
                k = U0["pool"] + j
                sp.wait_ge(unit_done, k - SLOTS + 1)
                c = POOL_COL + 256 * (POOL_ORDER[j // 2])
                sp.dma_start(raw[:, k % SLOTS, :].rearrange("p (kt n) -> p kt n", n=256), v[j % 2, :, :, c:c + 256])\
                    .then_inc(raw_in[k % SLOTS], 16)
            for j in range(2):
                u = U0["wpool"] + j
                sp.wait_ge(unit_done, u - SLOTS + 1)
                sp.dma_start(raw[:, u % SLOTS, :].rearrange("p (g kt n) -> p g kt n", g=2, kt=2),
                             A["w_pool"][2 - 2 * j:4 - 2 * j].rearrange("g (kt p) n -> p g kt n", p=P))\
                    .then_inc(raw_in[u % SLOTS], 16)
            v = A["w_in"].rearrange("(h kt p) (n) -> h p kt n", p=P, kt=8)
            with sp.Fori(0, 4) as i:
                for j in range(8):
                    k = U0["merge"] + j
                    sp.wait_ge(unit_done, i * 8 + (k - SLOTS + 1))
                    c = MERGE_COL + (j // 4) * D + ((j // 2) % 2) * 256
                    sp.dma_start(raw[:, k % SLOTS, :].rearrange("p (kt n) -> p kt n", n=256),
                                 v[j % 2, :, :, ds(i * 512 + c, 256)]).then_inc(raw_in[k % SLOTS], 16)
            pair_units("wout", A["w_out"], 0, 8)
            vg, vu = (A[n].rearrange("e (h kt p) n -> h p e kt n", p=P, kt=8) for n in ("w_expert_gate", "w_expert_up"))
            with sp.Fori(0, NEXP) as i:
                for j in range(4):
                    k = U0["experts"] + j
                    sp.wait_ge(unit_done, i * 4 + (k - SLOTS + 1))
                    sp.dma_start(raw[:, k % SLOTS, :].rearrange("p (kt n) -> p kt n", n=256),
                                 (vg if j < 2 else vu)[j % 2, :, ds(i, 1), :, :].rearrange("p e kt n -> p (e kt) n"))\
                        .then_inc(raw_in[k % SLOTS], 16)
            pair_units("down", A["w_expert_down"], 0, 8)
            v = A["a_w_in"].rearrange("(h kt p) n -> h p kt n", p=P, kt=8)
            vo = A["a_w_out"].rearrange("(q kt p) n -> q p kt n", p=P, kt=4)
            for u in range(60):
                k = U0["a_in"] + u
                sp.wait_ge(unit_done, k - SLOTS + 1)
                g = {5: 0, 15: 1, 20: 2, 25: 3}.get(u)
                if g is not None:
                    if g:
                        sp.wait_ge(rg_mm, SUP * g)
                    else:
                        sp.wait_ge(band_clear, 1)
                    for a, m, r0, r1 in BPIECES:
                        c = BOFF[a] + RBLK * m - BC[a]
                        sp.dma_start(band[r0 - P * a:r1 - P * a, :, c:c + RBLK],
                                     A["a_w_ri"][:, 4 * g + m, r0 - RBLK * m:r1 - RBLK * m, :].rearrange("j r c -> r j c"))\
                            .then_inc(band_in, 16)
                if u < 40:
                    c = (D_RNN if u < 20 else 0) + 256 * (u % 20 // 2)
                    src, n = v[u % 2, :, :, c:c + 256], 256
                else:
                    src, n = vo[(u - 40) % 5, :, :, 512 * ((u - 40) // 5):512 * ((u - 40) // 5) + 512], 512
                sp.dma_start(raw[:, k % SLOTS, :].rearrange("p (kt n) -> p kt n", n=n), src)\
                    .then_inc(raw_in[k % SLOTS], 16)

            def mlp(name, layer):
                w1, w2 = A["mlp_w1"][D * layer:D * layer + D, :], A["mlp_w2"][D_FF * layer:D_FF * layer + D_FF, :]
                for c in range(4):
                    pair_units(name, w1, CHUNK * c, 8, 32 * c)
                    pair_units(name, w2[CHUNK * c:CHUNK * c + CHUNK, :], 0, 8, 32 * c + 16)

            mlp("mlp0", 0)
            pair_units("v", A["w_kv"], D, 8)
            pair_units("k", A["w_kv"], 0, 8)
            pair_units("q", A["w_q"], 0, 8)
            v = A["w_o"].rearrange("(h kt p) n -> h p kt n", p=P, kt=8)
            for j, (pair, h) in enumerate(((0, 0), (1, 0), (0, 1), (1, 1))):
                k = U0["o"] + j
                sp.wait_ge(unit_done, k - SLOTS + 1)
                sp.dma_start(raw[:, k % SLOTS, :].rearrange("p (kt n) -> p kt n", n=256),
                             v[h, :, :, 256 * pair:256 * pair + 256]).then_inc(raw_in[k % SLOTS], 16)
            pair_units("o", A["w_o"], 512, 6, 4)
            mlp("mlp1", 1)
            for j in range(4):
                sp.wait_ge(result_ready, j + 1)
                sp.dma_start(out.rearrange("(kt p) t -> p kt t", p=P)[:, 4 * j:4 * j + 4, :], result[:, 4 * j:4 * j + 4, :])\
                    .then_inc(stored, 16)
            sp.wait_ge(stored, 64)

        @block.tensor
        def _(pe):
            def unit(u, slot, half, nhalf, pair, rh, rl, mid=None, free=None, need=None):
                pe.wait_ge(lo_ready, u + 1)
                if half == 0 and free is not None:
                    pe.wait_ge(acc_free, free)
                hw = high[:, slot, :].rearrange("p (kt n) -> p kt n", n=256)
                lw = low[:, slot, :].rearrange("p (kt n) -> p kt n", n=256)
                for n in range(2):
                    for k in range(8):
                        kt = 8 * half + k
                        if need is not None and n == 0:
                            need(kt)
                        h, l = rh(kt), rl(kt)
                        o = acc[:, 2 * (pair % 2) + n, 0:h.shape[-1]]
                        first, last = kt == 0, kt == 8 * nhalf - 1
                        c = slice(P * n, P * n + P)
                        pe.matmul(o, hw[:, k, c], h, start=first, stop=False)
                        pe.matmul(o, hw[:, k, c], l, start=False, stop=False)
                        m = pe.matmul(o, lw[:, k, c], h, start=False, stop=last)
                    if n == 0 and mid is not None:
                        mid()
                m.then_inc(unit_done, 1)

            def need_g(base):
                def need(kt):
                    if kt % 2 == 0:
                        pe.wait_ge(g_lo, base + kt // 2 + 1)
                return need

            x1 = (lambda kt: gh1[:, kt, :]), (lambda kt: gl1[:, kt, :])

            def pairs_stage(name, npairs, nhalf, rh, rl, first=None, hook=None, b_off=0, u_off=0, mid=None):
                n = npairs // 2

                def body(i):
                    fresh = isinstance(i, int) and i == 0 and (first is not None or hook is not None)
                    for pr in range(2):
                        for h in range(nhalf):
                            k = U0[name] + u_off + pr * nhalf + h
                            b = B0[name] + b_off + pr
                            unit(i * (2 * nhalf) + k, k % SLOTS, h, nhalf, b, rh, rl, free=i * 2 + (b - 1),
                                 need=first if fresh and pr == 0 else None, mid=mid if fresh and k == U0[name] else None)
                            if fresh and pr == 0 and h == 0 and hook is not None:
                                hook()
                peel = first is not None or hook is not None
                lo = int(peel)
                if peel:
                    body(0)
                with pe.Fori(0, n - lo) as i:
                    body(i + lo if lo else i)

            pe.wait_ge(setup, 1)
            unit(0, 0, 0, 2, 0, *x1, free=None, need=need_g(0))

            def first_stats():
                pe.wait_ge(x_summed, 1)
                pe.matmul(psx[:, 0, 0:S], ones[:, :], sqsum[:, 0:S], start=True, stop=True)
                for i in range(2):
                    m = pe.matmul(psx[:, 1, i:i + 1], sqsum[:, P * i:P * i + P], ones[:, 0:1], start=True, stop=True)
                m.then_inc(stat_mm, 1)

            def gate_logits():
                pe.wait_ge(wg_scaled, 1)
                for i in range(2):
                    for kt in range(KT):
                        m = pe.matmul(psx[:, 2 + i, 0:HEADS * NB], hT[:, kt, META + P * i:META + P * i + P],
                                      wgate[:, kt, :], start=kt == 0, stop=kt == KT - 1)
                m.then_inc(gate_mm, 1)

            def head_squares(p, m):
                pe.wait_ge(head_sq, m + 1)
                if m == 0:
                    pe.wait_ge(stat_rt, 1)
                pe.matmul(psx[:, 0, :], hones, xsq[:, :, :].rearrange("p a t -> p (a t)"), start=True, stop=True)\
                    .then_inc(head_mm, 1)

            def head_rotate(m):
                pe.wait_ge(head_n, m + 1)
                if m == 0:
                    pe.wait_ge(stat_rt, 1)
                pe.matmul(psx[:, 1, :], rot, xn[:, :, :].rearrange("p a t -> p (a t)"), start=True, stop=True)\
                    .then_inc(head_rot, 1)

            def spread(src, n):
                if n:
                    pe.wait_ge(aux_taken, n)
                else:
                    pe.wait_ge(gate_z, 1)
                for g in range(NKV):
                    m = pe.matmul(psx[:, 2 + g // 2, 256 * (g % 2):256 * (g % 2) + 256], dup[g % 2],
                                  src[:, g // 2, :], start=True, stop=True)
                m.then_inc(raw_aux, 1)

            def turn_values(p, n):
                pe.wait_ge(acc_free, p + 1)
                pe.wait_ge(aux_taken, n)
                for i in range(2):
                    for j in range(2):
                        m = pe.transpose(psx[:, 2, 256 * i + P * j:256 * i + P * j + P],
                                         xp[:, p % 2, j, P * i:P * i + P], ident)
                m.then_inc(raw_aux, 1)

            def compress_hidden():
                pe.wait_ge(cw_in, 32)
                for j in range(2):
                    for m2 in range(2):
                        for kt in range(KT):
                            m = pe.matmul(psx[:, 3, 60 * (2 * j + m2):60 * (2 * j + m2) + 60],
                                          cw1[j][:, kt, P * m2:P * m2 + P],
                                          flat[:, j, kt, :, :].rearrange("p g n -> p (g n)"),
                                          start=kt == 0, stop=kt == KT - 1)
                m.then_inc(chid_mm, 1)

            def compress_out():
                pe.wait_ge(chid_act, 2)
                pe.wait_ge(head_s, 6)
                for kt in range(2):
                    m = pe.matmul(psx[:, 1, 0:60], par("w2k", P * kt, P * kt + P), chid[:, 0, kt, :],
                                  start=kt == 0, stop=kt == 1)
                pe.wait_ge(aux_taken, 6)
                for g in range(NKV):
                    for kt in range(2):
                        m = pe.matmul(psx[0:NCMP, 2, HD * g:HD * g + HD],
                                      chid[:, 1, kt, NCMP * g:NCMP * g + NCMP],
                                      par("w2v", HD * kt, HD * kt + HD), start=kt == 0, stop=kt == 1)
                m.then_inc(kc_mm, 1)

            def compress_squares():
                pe.wait_ge(kc_sq, 1)
                pe.matmul(psx[:, 0, 0:60], hones, ck[:, 1, :], start=True, stop=True).then_inc(kc_ss, 1)

            def compress_rotate():
                pe.wait_ge(kc_n, 1)
                pe.matmul(psx[:, 1, 0:60], rot, ck[:, 2, :], start=True, stop=True).then_inc(kc_rot, 1)

            normed = {0: 0, 1: 1, 2: 2, 3: 3, 6: 4, 8: 5}
            after = {1: [first_stats], 2: [gate_logits]}
            for p, m in normed.items():
                after.setdefault(2 * p + 2, []).append(lambda p=p, m=m: head_squares(p, m))
                after.setdefault(2 * p + 4, []).insert(0, lambda m=m: head_rotate(m))
            for n, p in ((0, 4), (1, 5)):
                after.setdefault(2 * p + 2, []).append(
                    lambda p=p, n=n: (pe.wait_ge(acc_free, p + 1), spread(xp[:, p % 2, :, :], n)))
            after.setdefault(16, []).append(lambda: turn_values(7, 2))
            after.setdefault(17, []).append(lambda: (pe.wait_ge(head_done, 5), spread(krope, 3)))
            after.setdefault(20, []).append(lambda: turn_values(9, 4))
            after.setdefault(19, []).append(lambda: (pe.wait_ge(aux_taken, 4), compress_hidden()))
            after.setdefault(21, []).append(lambda: (pe.wait_ge(head_done, 6), pe.wait_ge(chid_act, 2), spread(krope, 5)))
            after.setdefault(23, []).append(compress_out)
            after.setdefault(24, []).append(compress_squares)
            after.setdefault(25, []).append(compress_rotate)
            for u in range(28):
                if u:
                    p = u // 2
                    unit(u, u % SLOTS, u % 2, 2, p, *x1, free=p - 1 if p > 1 else None,
                         need=need_g(0) if u == 1 else None)
                for f in after.get(u, []):
                    f()

            for j in range(2):
                u = U0["wpool"] + j
                slot = u % SLOTS
                pe.wait_ge(lo_ready, u + 1)
                hw, lw = (x[:, slot, :].rearrange("p (g kt n) -> p g kt n", g=2, kt=2) for x in (high, low))
                for g in range(2):
                    pe.wait_ge(pooled_lo, 2 * j + g + 1)
                    for n in range(4):
                        b = B0["wpool"] + 4 * j + 2 * g + n // 2
                        if n % 2 == 0:
                            pe.wait_ge(acc_free, b - 1)
                        o = acc[:, 2 * (b % 2) + n % 2, 0:S]
                        for kt in range(2):
                            t, c = 2 * POOL_ORDER[2 * j + g] + kt, slice(P * n, P * n + P)
                            pe.matmul(o, hw[:, 1 - g, kt, c], ph[:, t, :], start=kt == 0, stop=False)
                            pe.matmul(o, hw[:, 1 - g, kt, c], pl[:, t, :], start=False, stop=False)
                            m = pe.matmul(o, lw[:, 1 - g, kt, c], ph[:, t, :], start=False, stop=kt == 1)
                        if n % 2 == 1:
                            if g == 1 and n == 3:
                                m.then_inc(unit_done, 1)
                            else:
                                m.then_inc(wp_half, 1)

            def scores(g, i, r0):
                K = P * (i + 1)
                n = 2 * (2 * g + i) + r0 // 2
                if n == 0:
                    pe.wait_ge(mask_ready, 1)
                    pe.wait_ge(head_done, 6)
                    pe.wait_ge(kc_done, 2)
                    pe.wait_ge(aux_taken, 6)
                    pe.wait_ge(stat_rt, 1)
                if r0 == 2:
                    pe.wait_ge(s_exp, n)
                elif i == 0 and g > 0:
                    pe.wait_ge(pt_out, 8 * g)
                elif i == 1 and g > 0:
                    pe.wait_ge(ho_out, g)
                elif i == 1:
                    pe.wait_ge(pt_out, 3)
                if n and r0 == 0:
                    pe.wait_ge(o_out, 2 * g + i)
                for r in (r0, r0 + 1):
                    h = HPK * g + r
                    half = slice(HD * (r % 2), HD * (r % 2) + HD)
                    q = qT[half, h // 2, P * i:P * i + P]
                    for b in range(2):
                        pe.matmul(psx[:, r % 2, 256 * b:256 * b + K], q, kdup[half, b, g, 0:K], start=True, stop=False)
                        pe.matmul(psx[:, r % 2, 256 * b + P * i:256 * b + P * i + P], ident16, causal16,
                                  start=False, stop=True)
                    c = psx[:, 2 + r % 2, 16 * (r // 2):16 * (r // 2) + NCMP]
                    pe.matmul(c, q, kcT[half, g, :], start=True, stop=False)
                    m = pe.matmul(c, ident16, cmp16[:, 16 * i:16 * i + NCMP], start=False, stop=True)
                m.then_inc(s_mm, 1)

            def turn(g, i, j):
                n = 8 * g + (3 if i else 0) + j
                b, c, _, K = blocks_of(i)[j]
                pe.wait_ge(p_scaled, 4 * (2 * g + i) + 4)
                if j >= 2:
                    pe.wait_ge(pt_out, n - 1)
                for r in range(HPK):
                    m = pe.transpose(psx[0:K, j % 2, P * r:P * r + P], probs[:, r, c:c + K], ident)
                m.then_inc(pt_mm, 1)

            def values(g, i, j):
                n = 8 * g + (3 if i else 0) + j
                b, _, k, K = blocks_of(i)[j]
                v = vcT[:, g, :] if b == 2 else vtok[:, b, k, HD * g:HD * g + HD]
                pe.wait_ge(pt_out, n + 1)
                m = pe.matmul(psx[0:HD, 3, :], v, pts[0:K, n % 2, :], start=j == 0, stop=j == NT[i] - 1)
                m.then_inc(o_mm, 1)

            def heads_out(g):
                pe.wait_ge(o_out, 2 * g + 2)
                pe.wait_ge(wh_in, 16)
                pe.wait_ge(pt_out, 8 * g + (11 if g < 3 else 8))
                for r in range(HPK):
                    m = pe.matmul(psx[:, r // 2, 256 * (r % 2):256 * (r % 2) + 256], wh[:, HPK * g + r, :],
                                  og[:, r, :], start=True, stop=True)
                m.then_inc(ho_mm, 1)

            def slot_work(g, i, s):
                if s in (0, 2):
                    scores(g, i, s)
                elif s == 4:
                    turn(g, i, 0), turn(g, i, 1)
                elif s == 5:
                    values(g, i, 0), values(g, i, 1), turn(g, i, 2)
                    if i:
                        turn(g, i, 3)
                elif s == 6:
                    values(g, i, 2)
                    if i:
                        values(g, i, 3), turn(g, i, 4)
                elif s == 7:
                    if i:
                        values(g, i, 4)
                    elif g:
                        heads_out(g - 1)

            for g in range(NKV):
                for j in range(8):
                    u = U0["merge"] + 8 * g + j
                    i, s = j // 4, 2 * (j % 4)
                    slot_work(g, i, s)
                    b = B0["merge"] + 4 * g + j // 2
                    unit(u, u % SLOTS, j % 2, 2, b, *x1, free=b - 1, mid=lambda: slot_work(g, i, s + 1))

            def need_y(kt):
                if kt % 2 == 0:
                    pe.wait_ge(y_lo, kt // 2 + 1)

            pairs_stage("wout", 8, 2, lambda kt: yh[:, kt, :], lambda kt: yl[:, kt, :], first=need_y,
                        mid=lambda: heads_out(NKV - 1))

            def stats(r, T, by_token=False):
                pe.wait_ge(sq_used, 8 * r + 2)
                m = pe.matmul(psx[:, 0, 0:T], ones[:, :], sqsum[:, 0:T], start=True, stop=True)
                if by_token:
                    for i in range(2):
                        m = pe.matmul(psx[:, 1, i:i + 1], sqsum[:, P * i:P * i + P], ones[:, 0:1], start=True, stop=True)
                m.then_inc(stat_mm, 1)

            def router():
                stats(1, S, True)
                pe.wait_ge(rg_ready, 1)
                for i in range(2):
                    for kt in range(KT):
                        m = pe.matmul(psx[:, 2, 32 * i:32 * i + 20], hT[:, kt, META + P * i:META + P * i + P],
                                      rg[:, kt, :], start=kt == 0, stop=kt == KT - 1)
                m.then_inc(rl_mm, 1)

            def turn_weights():
                pe.wait_ge(comb_done, 1)
                for i in range(2):
                    m = pe.transpose(psx[0:NEXP, 3, P * i:P * i + P], comb[:, i, :], ident)
                m.then_inc(comb_t, 1)

            def weights_out(n):
                if n:
                    pe.wait_ge(wt_out, 1)
                else:
                    pe.wait_ge(comb_c, 1)
                for e in range(8 * n, 8 * n + 8):
                    m = pe.matmul(psx[:, (e % 8) // 2, 256 * (e % 2):256 * (e % 2) + 256],
                                  par("ident")[0:NEXP, e:e + 1].to_broadcast([NEXP, P]), combT[:, :], start=True, stop=True)
                    if e % 8 == 7:
                        m.then_inc(wt_mm, 1)

            def expert(i):
                for j in range(4):
                    k = U0["experts"] + j
                    fresh = isinstance(i, int)
                    unit(i * 4 + k, k % SLOTS, j % 2, 2, B0["experts"] + j // 2, lambda kt: gh2[:, kt, :],
                         lambda kt: gl2[:, kt, :], free=i * 2 + (B0["experts"] + j // 2 - 1),
                         need=need_g(8) if fresh and j < 2 else None, mid=turn_weights if fresh and j == 2 else None)
                    if fresh and j == 0:
                        router()
                    if fresh and j >= 2:
                        weights_out(j - 2)

            expert(0)
            with pe.Fori(0, NEXP - 1) as i:
                expert(i + 1)

            def need_hid(base):
                def need(kt):
                    if kt % 2 == 0:
                        pe.wait_ge(hid_lo, base + kt // 2 + 1)
                return need

            pairs_stage("down", 8, 4, lambda kt: hidh[:, kt, :], lambda kt: hidl[:, kt, :], first=need_hid(0))

            def out_tiles(u, slot, h, l, lo_kt, nkt, banks, first, last):
                pe.wait_ge(lo_ready, u + 1)
                hw, lw = (x[:, slot, :].rearrange("p (kt n) -> p kt n", kt=nkt) for x in (high, low))
                for n in range(4):
                    for k in range(nkt):
                        kt, c = lo_kt + k, slice(P * n, P * n + P)
                        if n == 0 and u < U0["a_out"] + 5 and kt % 2 == 0:
                            pe.wait_ge(ry_lo, kt // 2 + 1)
                        o = banks[:, n, 0:TB]
                        pe.matmul(o, hw[:, k, c], h[:, kt, :], start=first and k == 0, stop=False)
                        pe.matmul(o, hw[:, k, c], l[:, kt, :], start=False, stop=False)
                        m = pe.matmul(o, lw[:, k, c], h[:, kt, :], start=False, stop=last and k == nkt - 1)
                m.then_inc(unit_done, 1)

            def gate_blocks(t):
                g, b = t // SUP, t % SUP
                if b == 0:
                    pe.wait_ge(band_in, 16 * len(BPIECES) * (g + 1))
                pe.wait_ge(xr_done, min(t + 1, SUP * g + SUP - 1) // 2 + 1)
                if t >= 2:
                    pe.wait_ge(rg_sig, t - 1)
                meets = [a for a in range(SUP) if BC[a] <= P * b < BC[a] + BWID[a]]
                for j in range(2):
                    for a in meets:
                        c = BOFF[a] + P * b - BC[a]
                        m = pe.matmul(psx[:, 2 * j + t % 2, 0:TB], band[:, j, c:c + P], xr[:, SUP * g + a, :],
                                      start=a == meets[0], stop=a == meets[-1])
                m.then_inc(rg_mm, 1)

            for u in range(40):
                k = U0["a_in"] + u
                b = B0["a_in"] + u // 2
                unit(k, k % SLOTS, u % 2, 2, b, lambda kt: gh3[:, kt, :], lambda kt: gl3[:, kt, :], free=b - 1,
                     need=need_g(16) if u < 2 else None)
                if u == 0:
                    stats(2, TB)
                if 7 <= u < 7 + RT:
                    gate_blocks(u - 7)
            for u in range(20):
                g = u // 5
                if u % 5 == 0:
                    if g == 0:
                        pe.wait_ge(rg_sig, RT)
                    else:
                        pe.wait_ge(acc_free, B0["a_out"] + 2 * (g - 1))
                out_tiles(U0["a_out"] + u, (U0["a_out"] + u) % SLOTS, rh3, rl3, 4 * (u % 5), 4,
                          psx if g % 2 == 0 else acc, u % 5 == 0, u % 5 == 4)

            def mlp(name, r, split, h, l, T, base):
                for c in range(4):
                    pairs_stage(name, 8, 2, lambda kt: h[:, kt, 0:T], lambda kt: l[:, kt, 0:T],
                                first=need_g(8 * split) if c == 0 else None,
                                hook=(lambda: stats(r, T)) if c == 0 else None, b_off=16 * c, u_off=32 * c)
                    pairs_stage(name, 8, 2, lambda kt: fh[:, kt, 0:T], lambda kt: fl[:, kt, 0:T],
                                first=need_hid(base + 8 * c), b_off=16 * c + 8, u_off=32 * c + 16)

            mlp("mlp0", 3, 3, gh4, gl4, TB, NEXP)

            def turn_v(t):
                pe.wait_ge(acc_free, B0["v"] + t + 1)
                if t >= 2:
                    pe.wait_ge(v_out, t - 1)
                for j in range(2):
                    for k, (t0, n) in enumerate(TILES2):
                        at_ = 256 * k + P * j
                        m = pe.transpose(psx[0:n, 2 * (t % 2) + at_ // 512, at_ % 512:at_ % 512 + P],
                                         zb[:, t % 2, j, t0:t0 + n], ident)
                m.then_inc(v_mm, 1)

            def scores2(a):
                pe.wait_ge(q_done, a + 1)
                if a == 0:
                    pe.wait_ge(k_done, DH)
                    pe.wait_ge(v_out, DH)
                else:
                    pe.wait_ge(a_o, a)
                    pe.wait_ge(a_pt, a)
                for i in range(2):
                    K = META + P + P * i
                    for c in range(2):
                        o = psx[:, 0, K * c:K * c + K] if i == 0 else psx[:, 1 + c, 0:K]
                        pe.matmul(o, q2[:, a % 2, c, P * i:P * i + P], kT2[:, 2 * a + c, 0:K], start=True, stop=False)
                        m = pe.matmul(o[:, K - P:K], ident16, causal16, start=False, stop=True)
                m.then_inc(a_sc, 1)

            def turn2(a):
                pe.wait_ge(a_attn, a + 1)
                if a:
                    pe.wait_ge(a_rt, a)
                pe.transpose(psx[0:META, 3, 0:P], pr0[:, 0, 0:META], ident)
                pe.transpose(psx[0:META, 3, P:2 * P], pr1[:, 0, 0:META], ident)
                pe.transpose(psx[:, 3, 2 * P:3 * P], pr0[:, 0, META:META + P], ident)
                pe.transpose(psx[:, 3, 3 * P:4 * P], pr1[:, 0, META:META + P], ident)
                pe.transpose(psx[:, 0, 0:P], pr1[:, 0, META + P:TB], ident).then_inc(a_tr, 1)

            def values2(a):
                pe.wait_ge(a_pt, a + 1)
                for f in range(2):
                    o = psx[:, 1, S * f:S * f + S]
                    c = slice(2 * P * a + P * f, 2 * P * a + P * f + P)
                    pe.matmul(o, vt2[0:META, 0, c], pt2[0:META, 0:2, :].rearrange("p a t -> p (a t)"), start=True, stop=False)
                    pe.matmul(o, vt2[:, 1, c], pt2[:, 2:4, :].rearrange("p a t -> p (a t)"), start=False, stop=False)
                    m = pe.matmul(o[:, P:S], vt2[:, 2, c], pt2[:, 4, :], start=False, stop=True)
                m.then_inc(a_pv, 1)

            def squares2(a):
                pe.wait_ge(a_sq, a + 1)
                for f in range(2):
                    m = pe.matmul(psx[:, 3, 0:S], ones[:, :], osq[:, f, :], start=f == 0, stop=f == 1)
                m.then_inc(a_ss, 1)

            x5 = (lambda kt: gh5[:, kt, :]), (lambda kt: gl5[:, kt, :])
            x6 = (lambda kt: gh6[:, kt, :]), (lambda kt: gl6[:, kt, :])
            for u in range(48):
                k, b = U0["v"] + u, B0["v"] + u // 2
                a = (u - 32) // 2 - 1
                if u >= 34 and u % 2 == 0 and a >= 1:
                    values2(a - 1)

                def mid():
                    if u >= 34 and u % 2 == 0:
                        if a >= 1:
                            squares2(a - 1)
                        scores2(a)
                    elif u >= 34:
                        turn2(a)
                unit(k, k % SLOTS, u % 2, 2, b, *(x5 if u < 32 else x6), free=b - 1,
                     need=need_g(32) if u < 2 else need_g(40) if 32 <= u < 34 else None, mid=mid)
                if u == 0:
                    stats(4, TB)
                if u < 18 and u % 2 == 0 and u:
                    turn_v(u // 2 - 1)

            def need_o(kt):
                if kt % 2 == 0:
                    pe.wait_ge(o_lo, kt // 2 + 1)

            xo = (lambda kt: oh[:, kt, :]), (lambda kt: ol[:, kt, :])
            values2(DH - 2)
            for j, (pair, h) in enumerate(((0, 0), (1, 0), (0, 1), (1, 1))):
                k, b = U0["o"] + j, B0["o"] + pair
                if j == 2:
                    values2(DH - 1)
                    squares2(DH - 1)

                def mid():
                    if j == 0:
                        squares2(DH - 2)
                        scores2(DH - 1)
                    elif j == 1:
                        turn2(DH - 1)
                unit(k, k % SLOTS, h, 2, b, *xo, free=b - 1, need=need_o if pair == 0 else None, mid=mid)
            pairs_stage("o", 6, 2, *xo, b_off=2, u_off=4)
            mlp("mlp1", 5, 6, gh7, gl7, S, NEXP + 32)
            stats(6, S)

        @block.scalar
        def _(act):
            chain = Chain(act, chain_act)

            def hi(u, slot, turn):
                act.wait_ge(raw_in[slot], turn * 16 + 16)
                act.activation(high[:, slot, :], raw[:, slot, :], ACT.Copy).then_inc(hi_ready, 1)

            def hi_c(u):
                hi(u, u % SLOTS, u // SLOTS)

            act.dma_start(aux[:, :], A["aux"]).then_inc(aux_in, 16)
            act.wait_ge(aux_in, 16)
            for t in range(8):
                if t % 2 == 0:
                    act.wait_ge(x_in[t // 2], 16)
                for kt in (2 * t, 2 * t + 1):
                    m = act.activation(gh1[:, kt, :], hT[:, kt, TOK], ACT.Copy, scale=col("g_attn", kt))
                m.then_inc(g_hi, 1)
                if t == 3:
                    hi_c(0)
            act.dma_start(wgate[:, :, :], A["w_in"][:, GATE_COL:POOL_COL].rearrange("(kt p) n -> p kt n", p=P))\
                .then_inc(wg_in, 16)
            act.dma_start(mask32[:, :], A["mask"]).then_inc(mask_in, 16)
            act.dma_start(posi[:, :], A["positions"].to_broadcast([P, S]))\
                .then_inc(pos_in, 16)
            hi_c(1)
            act.activation(xsqr[:, :, :], hT[:, :, TOK], ACT.Square).then_inc(x_squared, 1)
            act.wait_ge(setup, 1)

            def first_root():
                act.wait_ge(stat_mm, 1)
                act.activation(inv[:, 0:S], psx[:, 0, 0:S], ACT.Sqrt, scale=1.0 / D, bias=eps)
                act.activation(invt, psx[:, 1, 0:2], ACT.Sqrt, scale=1.0 / D, bias=eps).then_inc(stat_rt, 1)

            def head_square(p, m):
                act.wait_ge(acc_free, p + 1)
                if m:
                    act.wait_ge(head_mm, m)
                act.activation(xsq[:, :, :], xp[:, p % 2, :, :], ACT.Square).then_inc(head_sq, 1)

            def head_root(m):
                act.wait_ge(head_mm, m + 1)
                if m:
                    act.wait_ge(head_n, m)
                act.activation(xrt[:, :, :].rearrange("p a t -> p (a t)"), psx[:, 0, :], ACT.Sqrt,
                               scale=1.0 / HD, bias=eps).then_inc(head_rt, 1)

            def take_keys(b, n):
                act.wait_ge(raw_aux, n + 1)
                act.activation(kdup[:, b, :, :].rearrange("p (a g) t -> p a (g t)", a=2), psx[:, 2:4, :], ACT.Copy)\
                    .then_inc(aux_taken, 1)

            def take_values(b, n):
                act.wait_ge(raw_aux, n + 1)
                act.activation(vtok[:, b, :, :].rearrange("p i d -> p (i d)"), psx[:, 2, :], ACT.Copy)\
                    .then_inc(aux_taken, 1)

            def gates_act():
                act.wait_ge(gate_z, 1)
                act.activation(gates[:, :, :, :], gates[:, :, :, :], ACT.Tanh, scale=0.5).then_inc(gates_tanh, 1)

            def chid_silu():
                act.wait_ge(chid_mm, 1)
                for j in range(2):
                    act.activation(chid[:, j, :, :].rearrange("p m c -> p (m c)"), psx[:, 3, 120 * j:120 * j + 120],
                                   ACT.Silu).then_inc(chid_act, 1)

            def kc_take():
                act.wait_ge(kc_mm, 1)
                act.activation(ck[:, 0, :], psx[:, 1, 0:60], ACT.Copy)
                act.activation(ck[:, 1, :], psx[:, 1, 0:60], ACT.Square).then_inc(kc_sq, 1)
                act.activation(vcT[:, :, :].rearrange("n g d -> n (g d)"), psx[0:NCMP, 2, 0:NKV * HD], ACT.Copy)\
                    .then_inc(kc_done, 1)

            def kc_root():
                act.wait_ge(kc_ss, 1)
                act.activation(ck[:, 3, :], psx[:, 0, 0:60], ACT.Sqrt, scale=1.0 / HD, bias=eps).then_inc(kc_rt, 1)

            def pool_hi(n):
                g = POOL_ORDER[n]
                act.wait_ge(pooled, n + 1)
                act.activation(ph[:, 2 * g:2 * g + 2, :], pw[:, 0, :, :], ACT.Copy).then_inc(pooled_hi, 1)

            def rope_tables():
                act.wait_ge(angle_ready, 1)
                act.activation(ropes[:, :], angle[:, 2, :], ACT.Sin)
                act.activation(ropec[:, :], angle[:, 3, :], ACT.Sin).then_inc(table_ready, 1)

            after = {0: [first_root], 2: [gates_act], 3: [rope_tables]}
            normed = {0: 0, 1: 1, 2: 2, 3: 3, 6: 4, 8: 5}
            for p, m in normed.items():
                after.setdefault(2 * p + 1, []).append(lambda p=p, m=m: head_square(p, m))
                after.setdefault(2 * p + 2, []).append(lambda m=m: head_root(m))
            after.setdefault(16, []).append(lambda: take_values(0, 2))
            after.setdefault(17, []).append(lambda: take_keys(0, 3))
            after.setdefault(20, []).extend([chid_silu, lambda: take_values(1, 4)])
            after.setdefault(21, []).append(lambda: take_keys(1, 5))
            after.setdefault(23, []).append(kc_take)
            after.setdefault(24, []).append(kc_root)
            for n, u in enumerate((24, 26, 27, 28)):
                after.setdefault(u, []).append(lambda n=n: pool_hi(n))
            for u in range(30):
                hi_c(u + 2)
                for f in after.get(u, []):
                    f()

            def exps(g, i, r0):
                n = 2 * (2 * g + i) + r0 // 2
                K = P * (i + 1)
                act.wait_ge(s_max, n + 1)
                if n >= 2:
                    act.wait_ge(pt_mm, 8 * g + (3 if i else 0))
                    act.wait_ge(coef, n - n % 2)
                for r in (r0, r0 + 1):
                    for b in range(2):
                        act.activation(probs[:, r, 256 * b:256 * b + K], psx[:, r % 2, 256 * b:256 * b + K], ACT.Exp,
                                       bias=stat[:, 2 * r + b:2 * r + b + 1],
                                       accum_out=stat[:, 12 + NB * r + 1 + b:12 + NB * r + 2 + b])
                    m = act.activation(probs[:, r, 512:512 + NCMP], psx[:, 2 + r % 2, 16 * (r // 2):16 * (r // 2) + NCMP],
                                       ACT.Exp, bias=stat[:, 8 + r:9 + r],
                                       accum_out=stat[:, 12 + NB * r:13 + NB * r])
                m.then_inc(s_exp, 1)

            def take_turned(g, i, j):
                n = 8 * g + (3 if i else 0) + j
                K = blocks_of(i)[j][3]
                act.wait_ge(pt_mm, n + 1)
                if n >= 2:
                    act.wait_ge(o_mm, n - 1)
                act.activation(pts[0:K, n % 2, :], psx[0:K, j % 2, :], ACT.Copy).then_inc(pt_out, 1)

            def take_o(g, i):
                act.wait_ge(o_mm, 8 * g + (8 if i else 3))
                if g:
                    act.wait_ge(ho_mm, g)
                act.activation(og[:, :, P * i:P * i + P], psx[0:HD, 3, :].rearrange("p (r t) -> p r t", r=HPK), ACT.Copy)\
                    .then_inc(o_out, 1)

            def merge_tanh(b):
                act.wait_ge(acc_free, B0["merge"] + b + 1)
                o = zb[:, b % 2, :, 0:S] if b % 4 >= 2 else ym[:, 4 * (b // 4) + 2 * (b % 4):4 * (b // 4) + 2 * (b % 4) + 2, :]
                act.activation(o, zb[:, b % 2, :, 0:S], ACT.Tanh, scale=0.5).then_inc(merge_t, 1)

            act.wait_ge(unit_done, U0["merge"])
            for g in range(NKV):
                for j in range(8):
                    u = U0["merge"] + 8 * g + j
                    i, s = j // 4, j % 4
                    if s == 0:
                        exps(g, i, 0)
                    elif s == 1:
                        exps(g, i, 2)
                    elif s == 2:
                        take_turned(g, i, 0), take_turned(g, i, 1)
                    elif i:
                        take_turned(g, i, 4)
                    hi_c(u + 2)
                    if s == 2:
                        take_turned(g, i, 2)
                        if i:
                            take_turned(g, i, 3)
                    elif s == 3 and not i:
                        take_o(g, 0)
                    if j == 7 and g < NKV - 1:
                        take_o(g, 1)
                    if j % 2:
                        merge_tanh(4 * g + j // 2)
            for t in range(8):
                if t == 3:
                    take_o(NKV - 1, 1)
                act.wait_ge(y_done, t // 2 + 1)
                act.wait_ge(unit_done, U0["wout"])
                act.activation(yh[:, 2 * t:2 * t + 2, :], ym[:, 2 * t:2 * t + 2, :], ACT.Copy, scale=0.5)\
                    .then_inc(y_hi, 1)

            def hi_loop(u, i, per):
                act.wait_ge(raw_in[u % SLOTS], i * (4 * per) + 16 * (u // SLOTS) + 16)
                act.activation(high[:, u % SLOTS, :], raw[:, u % SLOTS, :], ACT.Copy).then_inc(hi_ready, 1)

            def resid_stage(name, r, per, split, gain, gh, tok, last=False, u_off=0, b_off=0):
                T = tok.stop - tok.start

                def body(i):
                    for pr in range(2):
                        for j in range(per):
                            k = U0[name] + u_off + pr * per + j + 2
                            if not (isinstance(i, int) and i * 2 * per + k >= NUNITS):
                                hi_loop(k, i, 2 * per)
                        act.wait_ge(acc_free, i * 2 + (B0[name] + b_off + pr + 1))
                        resid(i * 2 + pr, i * 2 + pr, pr, r, split, gain, gh, tok)
                with act.Fori(0, 3 if last else 4) as i:
                    body(i)
                if last:
                    body(3)

            def resid(t, n, pr, r, split, gain, gh, tok):
                act.wait_ge(sq_used, n + (8 * (r - 1) + 1))
                act.activation(sq[:, pr, :, 0:tok.stop - tok.start], hT[:, ds(t * 2, 2), tok], ACT.Square).then_inc(sq_ready, 1)
                if gh is not None:
                    for k in range(2):
                        f = lambda x: x[:, ds(t * 2 + k, 1), :].rearrange("p a t -> p (a t)")
                        m = act.activation(f(gh), hT[:, ds(t * 2 + k, 1), tok].rearrange("p a t -> p (a t)"), ACT.Copy,
                                           scale=col(gain, t * 2 + k))
                    m.then_inc(g_hi, 1)

            def root(r, T, by_token=False):
                act.wait_ge(stat_mm, r + 1)
                m = act.activation(inv[:, 0:T], psx[:, 0, 0:T], ACT.Sqrt, scale=1.0 / D, bias=eps)
                if by_token:
                    m = act.activation(invt, psx[:, 1, 0:2], ACT.Sqrt, scale=1.0 / D, bias=eps)
                m.then_inc(stat_rt, 1)

            resid_stage("wout", 1, 2, 1, "g_ffn", gh2, TOK)

            hi_c(U0["experts"] + 2)
            root(1, S, True)
            hi_c(U0["experts"] + 3)
            act.wait_ge(comb_z, 1)
            act.activation(r4[:, 1, :, :], r4[:, 1, :, :], ACT.Exp).then_inc(comb_exp, 1)
            act.wait_ge(comb_z, 2)
            act.activation(r1[:, 4, :], r1[:, 4, :], ACT.Exp).then_inc(comb_exp, 1)
            act.wait_ge(comb_t, 1)
            act.activation(combT[:, :], psx[0:NEXP, 3, 0:S], ACT.Copy).then_inc(comb_c, 1)

            def expert(i):
                for j in range(4):
                    k = U0["experts"] + j + 2
                    if not (isinstance(i, int) and j < 2):
                        hi_loop(k, i, 4)
                    if j == 1:
                        act.wait_ge(acc_free, i * 2 + (B0["experts"] + 1))
                        act.activation(zb[:, 0, :, 0:S], zb[:, 0, :, 0:S], ACT.Silu).then_inc(silu_e, 1)
                act.wait_ge(hid_z, i + 1)
                act.activation(hidh[:, ds(i * 2, 2), :], zb[:, 1, :, 0:S], ACT.Copy).then_inc(hid_hi, 1)

            expert(0)
            with act.Fori(0, NEXP - 1) as i:
                expert(i + 1)
            resid_stage("down", 2, 4, 2, "g_a", gh3, ALL)

            hi_c(U0["a_in"] + 2)
            root(2, TB)
            act.wait_ge(lam_z, 1)
            act.activation(rc[:, 2, :], rc[:, 1, :], ACT.Exp, scale=-1.0).then_inc(lam_exp, 1)

            def gates_rt(k):
                q = slice(2 * (k % 2), 2 * (k % 2) + 2)
                if k == 0:
                    act.wait_ge(lam_z, 2)
                if k >= 2:
                    act.wait_ge(rg_b, k - 1)
                for t in (2 * k, 2 * k + 1):
                    act.wait_ge(rg_mm, t + 1)
                    act.activation(ri[:, t % 4, :], psx[:, 2 + t % 2, 0:TB], ACT.Sigmoid, bias=col("b_i", t))
                    act.activation(rr[:, t % 4, :], psx[:, t % 2, 0:TB], ACT.Sigmoid, bias=col("b_r", t)).then_inc(rg_sig, 1)
                for t in (2 * k, 2 * k + 1):
                    act.wait_ge(rg_sig, t + 1)
                    act.activation(ra[:, t % 4, :], rr[:, t % 4, :], ACT.Exp, scale=rc[:, 1, t:t + 1]).then_inc(rg_a, 1)
                for t in (2 * k, 2 * k + 1):
                    act.wait_ge(rg_a, t + 1)
                    act.activation(rr[:, t % 4, :], rr[:, t % 4, :], ACT.Tanh, scale=rc[:, 0, t:t + 1]).then_inc(rg_th, 1)
                act.wait_ge(rg_th, 2 * k + 2)
                act.activation(rr[:, q, :], rr[:, q, :], ACT.Sqrt, scale=-1.0).then_inc(rg_q, 1)

            def gelu(j):
                act.wait_ge(acc_free, B0["a_in"] + 10 + j + 1)
                act.activation(zb[:, j % 2, :, :], zb[:, j % 2, :, :], ACT.Gelu_apprx_tanh).then_inc(gelu_done, 1)

            def ry_high(j):
                act.wait_ge(ry_z, j + 1)
                act.activation(rh3[:, 2 * j:2 * j + 2, :], zb[:, j % 2, :, :], ACT.Copy).then_inc(ry_hi, 1)

            for u in range(60):
                k = (u - 9) // 2
                if u:
                    hi_c(U0["a_in"] + u + 2)
                if u % 2 and 0 <= k < RT // 2:
                    gates_rt(k)
                if u >= 21 and u < 40 and u % 2:
                    gelu((u - 21) // 2)
                if u >= 22 and u <= 40 and u % 2 == 0:
                    ry_high((u - 22) // 2)
                if u >= 40 and (u - 40) % 5 == 4:
                    for p in (0, 1):
                        t = 2 * ((u - 40) // 5) + p
                        act.wait_ge(acc_free, B0["a_out"] + t + 1)
                        resid(t, t, p, 3, 3, "g_mlp0", gh4, ALL)

            def plain_stage(name, u_off, n):
                with act.Fori(0, n // 4) as i:
                    for j in range(4):
                        hi_loop(U0[name] + u_off + j + 2, i, 4)

            def mlp(name, r, T, base, nxt, last=False):
                for c in range(4):
                    def body(i):
                        for pr in range(2):
                            for j in range(2):
                                k = U0[name] + 32 * c + 2 * pr + j + 2
                                if not (isinstance(i, int) and pr == 0 and j == 0):
                                    hi_loop(k, i, 4)
                            z = zb[:, pr, :, 0:T]
                            act.wait_ge(acc_free, i * 2 + (B0[name] + 16 * c + pr + 1))
                            act.activation(z, z, ACT.Square).then_inc(hid_sq, 1)
                            act.wait_ge(hid_sq, i * 2 + (base - NEXP + 8 * c + pr + 1))
                            act.activation(fh[:, ds(i * 4 + 2 * pr, 2), 0:T], z, ACT.Copy).then_inc(hid_hi, 1)
                    if c == 0:
                        hi_c(U0[name] + 2)
                        root(r, T)
                        body(0)
                    with act.Fori(0, 3 if c == 0 else 4) as i:
                        body(i + 1 if c == 0 else i)
                    if c < 3:
                        plain_stage(name, 32 * c + 16, 16)
                    else:
                        resid_stage(name, *nxt, last=last, u_off=112, b_off=56)

            mlp("mlp0", 3, TB, NEXP, (4, 2, 4, "g_kv", gh5, ALL))

            def take_v(t):
                act.wait_ge(v_mm, t + 1)
                c = slice(256 * t, 256 * t + 256)
                act.activation(vt2[0:META, 0, c], psx[0:META, 2 * (t % 2), 0:256], ACT.Copy)
                act.activation(vt2[:, 1:3, c],
                               psx[:, 2 * (t % 2):2 * (t % 2) + 2, :].rearrange("p a c -> p (a c)")[:, 256:768]
                               .rearrange("p (k c) -> p k c", k=2), ACT.Copy).then_inc(v_out, 1)

            def exps2(a):
                act.wait_ge(a_max, a + 1)
                if a:
                    act.wait_ge(a_tr, a)
                for i in range(2):
                    K = META + P + P * i
                    for c in range(2):
                        src = psx[:, 0, K * c:K * c + K] if i == 0 else psx[:, 1 + c, 0:K]
                        n = 2 * i + c
                        m = act.activation((pr0 if i == 0 else pr1)[:, c, :], src, ACT.Exp, bias=st2[:, n:n + 1],
                                           accum_out=st2[:, 4 + n:5 + n])
                m.then_inc(a_exp, 1)

            def take_turned2(a):
                act.wait_ge(a_tr, a + 1)
                if a:
                    act.wait_ge(a_pv, a)
                f = lambda x: x.rearrange("p a t -> p (a t)")
                act.activation(f(pt2[0:META, 0:2, :]), psx[0:META, 3, 0:2 * P], ACT.Copy)
                act.activation(f(pt2[:, 2:4, :]), psx[:, 3, 2 * P:4 * P], ACT.Copy)
                act.activation(pt2[:, 4, :], psx[:, 0, 0:P], ACT.Copy).then_inc(a_pt, 1)

            def square2(a):
                act.wait_ge(a_o, a + 1)
                if a:
                    act.wait_ge(a_ss, a)
                act.activation(osq[:, :, :], oT[:, 2 * a:2 * a + 2, :], ACT.Square).then_inc(a_sq, 1)

            def root2(a):
                act.wait_ge(a_ss, a + 1)
                if a:
                    act.wait_ge(a_od, a)
                act.activation(ort[:, :], psx[:, 3, 0:S], ACT.Sqrt, scale=1.0 / (2 * HD2), bias=sub_eps).then_inc(a_rt, 1)

            for u in range(48):
                a = (u - 32) // 2 - 1
                if u == 32:
                    act.wait_ge(unit_done, U0["q"])
                    for t in range(8):
                        for kt in (2 * t, 2 * t + 1):
                            m = act.activation(gh6[:, kt, :], hT[:, kt, TOK], ACT.Copy, scale=col("g_b", kt))
                        m.then_inc(g_hi, 1)
                if u >= 34 and u % 2 == 0 and a:
                    square2(a - 1)
                hi_c(U0["v"] + u + 2)
                if u == 0:
                    root(4, TB)
                    act.wait_ge(dl_z, 1)
                    act.activation(st2[:, 16:18], st2[:, 12:14], ACT.Exp).then_inc(dl_exp, 1)
                if u and u < 18 and u % 2 == 0:
                    take_v(u // 2 - 1)
                if u >= 34:
                    if u % 2 == 0:
                        exps2(a)
                        if a:
                            root2(a - 1)
                    else:
                        take_turned2(a)

            def split_o(a):
                act.wait_ge(a_od, a + 1)
                act.activation(oh[:, 2 * a:2 * a + 2, :], oT[:, 2 * a:2 * a + 2, :], ACT.Copy).then_inc(o_hi, 1)

            act.wait_ge(unit_done, U0["o"])
            for a in range(DH - 2):
                split_o(a)
            for j in range(4):
                if j == 0:
                    square2(DH - 2)
                hi_c(U0["o"] + j + 2)
                if j == 0:
                    exps2(DH - 1)
                    root2(DH - 2)
                    split_o(DH - 2)
                elif j == 1:
                    take_turned2(DH - 1)
                    square2(DH - 1)
                    root2(DH - 1)
                    split_o(DH - 1)
            for t in range(2):
                act.wait_ge(acc_free, B0["o"] + t + 1)
                resid(t, t, t, 5, 6, "g_mlp1", gh7, TOK)

            def body(i):
                for pr in range(2):
                    for j in range(2):
                        hi_loop(U0["o"] + 4 + 2 * pr + j + 2, i, 4)
                    act.wait_ge(acc_free, i * 2 + (B0["o"] + 2 + pr + 1))
                    resid(i * 2 + (2 + pr), i * 2 + (2 + pr), pr, 5, 6, "g_mlp1", gh7, TOK)
            with act.Fori(0, 3) as i:
                body(i)
            mlp("mlp1", 5, S, NEXP + 32, (6, 2, 7, None, None, TOK), last=True)
            root(6, S)

        @block.vector
        def _(dve):
            chain = Chain(dve, chain_dve)
            link = chain.link

            def lo(u, slot):
                dve.wait_ge(hi_ready, u + 1)
                dve.tensor_tensor(low[:, slot, :], raw[:, slot, :], high[:, slot, :].bitcast(F32), ALU.subtract)\
                    .then_inc(lo_ready, 1)

            def lo_c(u):
                lo(u, u % SLOTS)

            def over2(ap):
                return ap.unsqueeze(1).to_broadcast([ap.shape[0], 2, ap.shape[-1]])

            dve.memset(small[:, 0:1], EPS)
            dve.memset(small[:, 1:2], SUB_EPS)
            dve.memset(ones[:, :], 1.0).then_inc(setup, 1)
            dve.wait_ge(aux_in, 16)
            def g_low(t, gain, gh, gl, tok, n):
                dve.wait_ge(g_hi, n)
                for k in range(2):
                    f = lambda x: x.rearrange("p a t -> p (a t)")
                    m = dve.scalar_tensor_tensor(f(gl[:, ds(t * 2 + k, 1), :]), f(hT[:, ds(t * 2 + k, 1), tok]),
                                                 col(gain, t * 2 + k), f(gh[:, ds(t * 2 + k, 1), :]).bitcast(F32),
                                                 ALU.mult, ALU.subtract)
                m.then_inc(g_lo, 1)

            for t in range(8):
                g_low(t, "g_attn", gh1, gl1, TOK, t + 1)
                if t == 3:
                    lo_c(0)
            lo_c(1)
            dve.wait_ge(x_squared, 1)
            dve.tensor_reduce(sqsum[:, 0:S], xsqr[:, :, :].rearrange("p k t -> p t k"), AX.X, ALU.add).then_inc(x_summed, 1)
            dve.wait_ge(mask_in, 16)
            dve.tensor_copy(maskb[:, :], mask32[:, :]).then_inc(mask_ready, 1)
            dve.wait_ge(wg_in, 16)
            dve.tensor_tensor(wgate[:, :, :], wgate[:, :, :],
                              par("g_attn").unsqueeze(2).to_broadcast([P, KT, HEADS * NB]), ALU.mult).then_inc(wg_scaled, 1)

            def first_inv():
                dve.wait_ge(stat_rt, 1)
                link(dve.reciprocal(inv[:, 0:S], inv[:, 0:S]))
                link(dve.reciprocal(invt, invt))
                link(dve.tensor_scalar(g_q8, par("g_q"), HD ** -0.5, None, ALU.mult))

            def angles():
                dve.wait_ge(pos_in, 16)
                link(dve.tensor_copy(angle[:, 0, :], posi[:, :]))
                link(dve.tensor_scalar(angle[:, 0, :], angle[:, 0, :], par("freq"), None, ALU.mult))
                link(dve.tensor_scalar(angle[:, 1, :], angle[:, 0, :], float(1 / (2 * np.pi)), None, ALU.mult))
                link(dve.tensor_scalar(angle[:, 1, :], angle[:, 1, :], ROUND, None, ALU.add))
                link(dve.tensor_scalar(angle[:, 1, :], angle[:, 1, :], -ROUND, None, ALU.add))
                for c in TWO_PI:
                    link(dve.scalar_tensor_tensor(angle[:, 0, :], angle[:, 1, :], -c, angle[:, 0, :], ALU.mult, ALU.add))
                dve.tensor_scalar(angle[:, 2, :], angle[:, 0, :], PI_IN, -PI_IN, ALU.min, ALU.max)
                link(dve.tensor_scalar(angle[:, 4, :], angle[:, 0, :], float(np.pi / 2), None, ALU.add))
                link(dve.tensor_scalar(angle[:, 5, :], angle[:, 4, :], float(np.pi), -float(2 * np.pi), ALU.is_gt, ALU.mult))
                link(dve.tensor_tensor(angle[:, 4, :], angle[:, 4, :], angle[:, 5, :], ALU.add))
                dve.tensor_scalar(angle[:, 3, :], angle[:, 4, :], PI_IN, -PI_IN, ALU.min, ALU.max).then_inc(angle_ready, 1)

            def take_pair(b, to):
                m = dve.tensor_tensor(to, acc[:, 2 * (b % 2):2 * (b % 2) + 2, 0:S], over2(inv[:, 0:S]), ALU.mult)
                return m

            def gate_take():
                dve.wait_ge(gate_mm, 1)
                for i in range(2):
                    m = dve.tensor_scalar(gates[:, i, :, :].rearrange("p h b -> p (h b)"), psx[:, 2 + i, 0:HEADS * NB],
                                          invt[:, i:i + 1], None, ALU.mult)
                m.then_inc(gate_z, 1)
                dve.wait_ge(gates_tanh, 1)
                link(dve.tensor_scalar(gates[:, :, :, :], gates[:, :, :, :], 0.5, 0.5, ALU.mult, ALU.add))
                link(dve.tensor_tensor(gates[:, :, :, 0], gates[:, :, :, 0],
                                       par("seen").unsqueeze(2).to_broadcast([P, 2, HEADS]), ALU.mult))

            def head_norm(p, m):
                g = g_q8 if m < 4 else par("g_ks") if m == 4 else par("g_kw")
                dve.wait_ge(head_rt, m + 1)
                link(dve.reciprocal(xrt[:, :, :], xrt[:, :, :]))
                if m:
                    dve.wait_ge(head_rot, m)
                    dve.wait_ge(head_done, m)
                dve.scalar_tensor_tensor(xn[:, :, :], xp[:, p % 2, :, :], g, xrt[:, :, :], ALU.mult, ALU.mult)\
                    .then_inc(head_n, 1)

            def head_sine(m):
                dve.wait_ge(head_rot, m + 1)
                if m:
                    dve.wait_ge(head_done, m)
                else:
                    dve.wait_ge(table_ready, 1)
                dve.tensor_tensor(xs[:, :, :], psx[:, 1, :].rearrange("p (a t) -> p a t", a=2), over2(ropes[:, :]), ALU.mult)\
                    .then_inc(head_s, 1)

            def flatten(j, n):
                dve.wait_ge(raw_aux, n + 1)
                pos = par("pos_k" if j == 0 else "pos_v")
                for g in range(NKV):
                    v = psx[:, 2 + g // 2, 256 * (g % 2):256 * (g % 2) + 256].rearrange("p (m c e) -> p e c m", c=8, e=2)
                    for e in range(2):
                        hp = slice(HD * e, HD * e + HD)
                        for k in range(2):
                            m = dve.tensor_tensor(flat[hp, j, 8 * k:8 * k + 8, g, :], v[hp, e, :, k:k + NCMP],
                                                  pos[hp, 8 * k:8 * k + 8].unsqueeze(2).to_broadcast([HD, 8, NCMP]), ALU.add)
                    if g == 3:
                        m.then_inc(aux_taken, 1)

            def kc_norm():
                dve.wait_ge(kc_rt, 1)
                link(dve.reciprocal(ck[:, 3, :], ck[:, 3, :]))
                dve.scalar_tensor_tensor(ck[:, 2, :], ck[:, 0, :], par("g_kc"), ck[:, 3, :], ALU.mult, ALU.mult).then_inc(kc_n, 1)

            def kc_rope():
                dve.wait_ge(kc_rot, 1)
                f = lambda x: x.rearrange("p (g n) -> p g n", g=NKV)
                at_end = lambda x: x.rearrange("p (n c) -> p c n", c=16)[:, 15, 1:16].unsqueeze(1).to_broadcast([P, NKV, NCMP])
                link(dve.tensor_tensor(f(ck[:, 3, :]), f(psx[:, 1, 0:60]), at_end(ropes[:, :]), ALU.mult))
                link(dve.tensor_tensor(f(ck[:, 0, :]), f(ck[:, 2, :]), at_end(ropec[:, :]), ALU.mult))
                dve.tensor_tensor(kcT[:, :, :], f(ck[:, 0, :]), f(ck[:, 3, :]), ALU.add).then_inc(kc_done, 1)

            def pool_low(n):
                g = POOL_ORDER[n]
                dve.wait_ge(pooled_hi, n + 1)
                dve.tensor_tensor(pl[:, 2 * g:2 * g + 2, :], pw[:, 0, :, :], ph[:, 2 * g:2 * g + 2, :].bitcast(F32),
                                  ALU.subtract).then_inc(pooled_lo, 1)

            after = {0: [first_inv], 2: [gate_take], 3: [angles]}
            normed = {0: 0, 1: 1, 2: 2, 3: 3, 6: 4, 8: 5}
            for p, m in normed.items():
                after.setdefault(2 * p + 2, []).append(lambda p=p, m=m: head_norm(p, m))
                after.setdefault(2 * p + 4, []).append(lambda m=m: head_sine(m))
            after.setdefault(10, []).append(lambda: flatten(0, 0))
            after.setdefault(12, []).append(lambda: flatten(1, 1))
            after.setdefault(24, []).append(kc_norm)
            after.setdefault(25, []).append(kc_rope)
            spread_at = {4: 1, 5: 2, 7: 3, 9: 5}
            for n in range(2):
                after.setdefault(24 + 2 * n, []).append(lambda n=n: pool_low(n))
            for u in range(28):
                lo_c(u + 2)
                for f in after.get(u, []):
                    f()
                if u % 2:
                    p = u // 2
                    dve.wait_ge(unit_done, u + 1)
                    if p - 2 in spread_at:
                        dve.wait_ge(raw_aux, spread_at[p - 2])
                    elif p >= 12:
                        dve.wait_ge(pooled, p - 11)
                    take_pair(p, xp[:, p % 2, :, :]).then_inc(acc_free, 1)

            pool_low(2)
            for j in range(2):
                lo_c(U0["wpool"] + j + 2)
                for q in range(4):
                    b = B0["wpool"] + 4 * j + q
                    if j == 0 and q == 2:
                        pool_low(3)
                    if q == 3:
                        dve.wait_ge(unit_done, U0["wpool"] + j + 1)
                    else:
                        dve.wait_ge(wp_half, 3 * j + q + 1)
                    for k in range(2):
                        t = 4 * POOL_ORDER[2 * j + q // 2] + 2 * (q % 2) + k
                        m = dve.tensor_scalar(pb[:, t, :], acc[:, 2 * (b % 2) + k, 0:S], col("pool_scale", t), None, ALU.mult)
                    m.then_inc(acc_free, 1)

            def maxima(g, i, r0):
                n = 2 * (2 * g + i) + r0 // 2
                K = P * (i + 1)
                dve.wait_ge(s_mm, n + 1)
                dve.tensor_reduce(stat[:, 2 * r0:2 * r0 + 4],
                                  psx[:, 0:2, :].rearrange("p a (b k) -> p (a b) k", b=2)[:, :, 0:K], AX.X, ALU.max, negate=True)
                dve.tensor_reduce(stat[:, 8 + r0:10 + r0], psx[:, 2:4, 8 * r0:8 * r0 + NCMP], AX.X, ALU.max, negate=True)\
                    .then_inc(s_max, 1)

            def weigh(g, i, r0):
                n, a, b = 2 * (2 * g + i) + r0 // 2, NB * r0, NB * r0 + 2 * NB
                dve.wait_ge(s_exp, n + 1)
                if n:
                    dve.wait_ge(p_scaled, 2 * n)
                link(dve.reciprocal(stat[:, 24 + a:24 + b], stat[:, 12 + a:12 + b]))
                dve.tensor_tensor(stat[:, 36 + a:36 + b], stat[:, 24 + a:24 + b],
                                  gates[:, i, HPK * g + r0:HPK * g + r0 + 2, :].rearrange("p h b -> p (h b)"), ALU.mult)\
                    .then_inc(coef, 1)
                dve.wait_ge(coef, n + 1)
                K = P * (i + 1)
                for r in (r0, r0 + 1):
                    pr = probs[:, r, 0:512].rearrange("p (b k) -> p b k", b=2)[:, :, 0:K]
                    c = stat[:, 36 + NB * r + 1:36 + NB * r + 3].unsqueeze(2).to_broadcast([P, 2, K])
                    dve.tensor_tensor(pr, pr, c, ALU.mult)
                    dve.tensor_scalar(probs[:, r, 512:512 + NCMP], probs[:, r, 512:512 + NCMP],
                                      stat[:, 36 + NB * r:37 + NB * r], None, ALU.mult).then_inc(p_scaled, 1)

            def take_merge(b):
                u = U0["merge"] + 2 * b + 2
                dve.wait_ge(unit_done, u)
                if b >= 2:
                    dve.wait_ge(merge_t, b - 1)
                take_pair(B0["merge"] + b, zb[:, b % 2, :, 0:S]).then_inc(acc_free, 1)

            def gate_pool(b):
                t = 4 * (b // 4) + 2 * (b % 4 - 2)
                dve.wait_ge(merge_t, b + 1)
                link(dve.scalar_tensor_tensor(pb[:, t:t + 2, :], zb[:, b % 2, :, 0:S], 1.0, pb[:, t:t + 2, :], ALU.add, ALU.mult))

            def merge_group(g):
                dve.wait_ge(ho_mm, g + 1)
                y = ym[:, 4 * g:4 * g + 4, :]
                dve.scalar_tensor_tensor(y, y, 1.0, psx[:, 0:2, :].rearrange("p a (b t) -> p (a b) t", b=2), ALU.add, ALU.mult)\
                    .then_inc(ho_out, 1)
                dve.wait_ge(ho_out, g + 1)
                dve.tensor_tensor(y, y, pb[:, 4 * g:4 * g + 4, :], ALU.add).then_inc(y_done, 1)

            for g in range(NKV):
                for j in range(8):
                    u = U0["merge"] + 8 * g + j
                    i, s = j // 4, j % 4
                    if s == 0:
                        maxima(g, i, 0)
                    elif s == 1:
                        maxima(g, i, 2)
                        weigh(g, i, 2)
                    lo_c(u + 2)
                    if s == 0:
                        weigh(g, i, 0)
                    if j == 3 and g:
                        merge_group(g - 1)
                    if j % 2:
                        take_merge(4 * g + j // 2)
                        if j >= 5:
                            gate_pool(4 * g + j // 2)
            for t in range(8):
                if t == 6:
                    merge_group(NKV - 1)
                dve.wait_ge(y_hi, t + 1)
                dve.scalar_tensor_tensor(yl[:, 2 * t:2 * t + 2, :], ym[:, 2 * t:2 * t + 2, :], 0.5,
                                         yh[:, 2 * t:2 * t + 2, :].bitcast(F32), ALU.mult, ALU.subtract).then_inc(y_lo, 1)

            def lo_loop(k, i, per):
                dve.wait_ge(hi_ready, i * per + (k + 1))
                dve.tensor_tensor(low[:, k % SLOTS, :], raw[:, k % SLOTS, :], high[:, k % SLOTS, :].bitcast(F32), ALU.subtract)\
                    .then_inc(lo_ready, 1)

            def resid_stage(name, per, split, gain, gh, gl, tok, add, last=False, u_off=0, b_off=0):
                T = add.stop - add.start

                def body(i):
                    for pr in range(2):
                        for j in range(per):
                            k = U0[name] + u_off + pr * per + j
                            if not (isinstance(i, int) and i * 2 * per + k + 2 >= NUNITS):
                                lo_loop(k + 2, i, 2 * per)
                        b = B0[name] + b_off + pr
                        dve.wait_ge(unit_done, i * (2 * per) + (k + 1))
                        h = hT[:, ds(i * 4 + 2 * pr, 2), add]
                        dve.tensor_tensor(h, h, acc[:, 2 * (b % 2):2 * (b % 2) + 2, 0:T], ALU.add).then_inc(acc_free, 1)
                        if gl is not None:
                            g_low(i * 2 + pr, gain, gh, gl, tok, i * 2 + (8 * split + pr + 1))
                with dve.Fori(0, 3 if last else 4) as i:
                    body(i)
                if last:
                    body(3)

            def root(r, T, by_token=False):
                dve.wait_ge(stat_rt, r + 1)
                link(dve.reciprocal(inv[:, 0:T], inv[:, 0:T]))
                if by_token:
                    link(dve.reciprocal(invt, invt))

            resid_stage("wout", 2, 1, "g_ffn", gh2, gl2, TOK, TOK)

            lo_c(U0["experts"] + 2)
            root(1, S, True)
            lo_c(U0["experts"] + 3)
            over4 = lambda x: x.unsqueeze(2).to_broadcast([P, 2, 4])
            tt, ts_ = (lambda o, a, b, op: link(dve.tensor_tensor(o, a, b, op))), dve.tensor_scalar
            order = par("order").rearrange("p (i e) -> p i e", i=2)
            peak = lambda o, x: link(dve.tensor_reduce(o, x, AX.X, ALU.max))

            def first_best(one_hot, key, x, best, top):
                peak(best, x)
                tt(key, x, over4(best), ALU.is_equal)
                tt(key, key, order, ALU.mult)
                peak(top, key)
                tt(one_hot, key, over4(top), ALU.is_equal)

            dve.wait_ge(rl_mm, 1)
            for i in range(2):
                link(dve.scalar_tensor_tensor(rl[:, i, :], psx[:, 2, 32 * i:32 * i + 20], invt[:, i:i + 1],
                                              par("router_b"), ALU.mult, ALU.add))
            group, e4 = r4[:, 0, :, :], r4[:, 1, :, :]
            first_best(group, r4[:, 2, :, :], rl[:, :, 0:4], r1[:, 0, :], r1[:, 1, :])
            dve.tensor_tensor(e4, rl[:, :, 0:4], over4(r1[:, 0, :]), ALU.subtract).then_inc(comb_z, 1)
            dve.wait_ge(comb_exp, 1)
            link(dve.tensor_reduce(r1[:, 2, :], e4, AX.X, ALU.add))
            link(dve.reciprocal(r1[:, 2, :], r1[:, 2, :]))
            for i in range(2):
                link(dve.tensor_tensor(r44[:, i, :, :], rl[:, i, 4:20].rearrange("p (g e) -> p g e", g=NGRP),
                                       group[:, i, :].unsqueeze(2).to_broadcast([P, NGRP, EPG]), ALU.mult))
                link(dve.tensor_reduce(r4[:, 3, i, :], r44[:, i, :, :].rearrange("p g e -> p e g"), AX.X, ALU.add))
            first_best(r4[:, 4, :, :], r4[:, 2, :, :], r4[:, 3, :, :], r1[:, 0, :], r1[:, 1, :])
            link(dve.scalar_tensor_tensor(r4[:, 3, :, :], r4[:, 4, :, :], NEG, r4[:, 3, :, :], ALU.mult, ALU.add))
            first_best(r4[:, 5, :, :], r4[:, 2, :, :], r4[:, 3, :, :], r1[:, 3, :], r1[:, 1, :])
            dve.tensor_tensor(r1[:, 4, :], r1[:, 3, :], r1[:, 0, :], ALU.subtract).then_inc(comb_z, 1)
            dve.wait_ge(comb_exp, 2)
            link(ts_(r1[:, 5, :], r1[:, 4, :], 1.0, None, ALU.add))
            link(dve.reciprocal(r1[:, 5, :], r1[:, 5, :]))
            tt(r1[:, 5, :], r1[:, 5, :], r1[:, 2, :], ALU.mult)
            tt(r1[:, 6, :], r1[:, 5, :], r1[:, 4, :], ALU.mult)
            tt(r4[:, 4, :, :], r4[:, 4, :, :], over4(r1[:, 5, :]), ALU.mult)
            tt(r4[:, 5, :, :], r4[:, 5, :, :], over4(r1[:, 6, :]), ALU.mult)
            tt(r4[:, 4, :, :], r4[:, 4, :, :], r4[:, 5, :, :], ALU.add)
            for i in range(2):
                m = dve.tensor_tensor(comb[:, i, :].rearrange("p (g e) -> p g e", g=NGRP),
                                      group[:, i, :].unsqueeze(2).to_broadcast([P, NGRP, EPG]),
                                      r4[:, 4, i, :].unsqueeze(1).to_broadcast([P, NGRP, EPG]), ALU.mult)
            m.then_inc(comb_done, 1)
            even = weight[:, :, :].rearrange("p (e two) t -> p e two t", two=2)[:, :, 0, :]

            def take_weights(n):
                dve.wait_ge(wt_mm, n + 1)
                dve.tensor_tensor(even[:, 8 * n:8 * n + 8, :], psx[:, :, :].rearrange("p a (b t) -> p (a b) t", b=2),
                                  inv[:, 0:S].unsqueeze(1).to_broadcast([P, 8, S]), ALU.mult).then_inc(wt_out, 1)

            def expert(i):
                fresh = isinstance(i, int)
                for j in range(4):
                    k = U0["experts"] + j
                    if not (fresh and j < 2):
                        lo_loop(k + 2, i, 4)
                    b = B0["experts"] + j // 2
                    src = acc[:, 2 * (b % 2):2 * (b % 2) + 2, 0:S]
                    if j == 1:
                        dve.wait_ge(unit_done, i * 4 + (k + 1))
                        dve.tensor_tensor(zb[:, 0, :, 0:S], src, over2(inv[:, 0:S]), ALU.mult).then_inc(acc_free, 1)
                    if j == 2 and fresh:
                        take_weights(0)
                dve.wait_ge(unit_done, i * 4 + (U0["experts"] + 4))
                if fresh:
                    dve.wait_ge(wt_out, 1)
                wt = weight[:, ds(i * 2, 1), :].to_broadcast([P, 2, S])
                dve.tensor_tensor(zb[:, 1, :, 0:S], src, wt, ALU.mult).then_inc(acc_free, 1)
                dve.wait_ge(silu_e, i + 1)
                dve.wait_ge(acc_free, i * 2 + (B0["experts"] + 2))
                dve.tensor_tensor(zb[:, 1, :, 0:S], zb[:, 1, :, 0:S], zb[:, 0, :, 0:S], ALU.mult).then_inc(hid_z, 1)
                dve.wait_ge(hid_hi, i + 1)
                dve.tensor_tensor(hidl[:, ds(i * 2, 2), :], zb[:, 1, :, 0:S], hidh[:, ds(i * 2, 2), :].bitcast(F32),
                                  ALU.subtract).then_inc(hid_lo, 1)

            expert(0)
            take_weights(1)
            dve.wait_ge(wt_out, 2)
            with dve.Fori(0, NEXP - 1) as i:
                expert(i + 1)
            resid_stage("down", 4, 2, "g_a", gh3, gl3, ALL, TOK)

            root(2, TB)
            lo_c(U0["a_in"] + 2)
            half_log, z, s_, s2, p_ = (rc[:, k, :] for k in (0, 2, 3, 4, 5))
            link(ts_(half_log, par("lam"), -1.0, None, ALU.mult))
            dve.tensor_tensor(rc[:, 1, :], half_log, par("lam"), ALU.max).then_inc(lam_z, 1)
            dve.wait_ge(lam_exp, 1)
            link(ts_(s_, z, 2.0, None, ALU.add))
            link(dve.reciprocal(s_, s_))
            tt(s_, s_, z, ALU.mult)
            tt(s2, s_, s_, ALU.mult)
            link(ts_(p_, s2, 1.0 / 17, 1.0 / 15, ALU.mult, ALU.add))
            for n in (13, 11, 9, 7, 5, 3, 1):
                tt(p_, p_, s2, ALU.mult)
                link(ts_(p_, p_, 1.0 / n, None, ALU.add))
            tt(p_, p_, s_, ALU.mult)
            link(ts_(half_log, half_log, 0.0, -4.0, ALU.max, ALU.mult))
            link(dve.memset(zp[:, :, :, 0:CONV - 1], 0.0))
            link(dve.scalar_tensor_tensor(half_log, p_, -8.0, half_log, ALU.mult, ALU.add))
            ts_(rc[:, 1, :], half_log, 2.0, None, ALU.mult).then_inc(lam_z, 1)

            def take_xr(p):
                b = B0["a_in"] + p
                dve.wait_ge(unit_done, U0["a_in"] + 2 * p + 2)
                z = zp[:, p % 2, :, :]
                dve.tensor_tensor(z[:, :, CONV - 1:CONV - 1 + TB], acc[:, 2 * (b % 2):2 * (b % 2) + 2, 0:TB],
                                  over2(inv[:, :]), ALU.mult).then_inc(acc_free, 1)
                dve.wait_ge(acc_free, b + 1)
                for tap in range(CONV):
                    for k in range(2):
                        t = 2 * p + k
                        if tap == 0:
                            m = ts_(xr[:, t, :], z[:, k, 0:TB], col("conv_w", t), col("conv_b", t), ALU.mult, ALU.add)
                        else:
                            m = dve.scalar_tensor_tensor(xr[:, t, :], z[:, k, tap:tap + TB], col("conv_w", RT * tap + t),
                                                         xr[:, t, :], ALU.mult, ALU.add)
                        if tap < CONV - 1 or k == 0:
                            link(m)
                m.then_inc(xr_done, 1)

            def decay(k):
                r, a = (x[:, 2 * (k % 2):2 * (k % 2) + 2, :] for x in (rr, ra))
                dve.wait_ge(rg_q, k + 1)
                dve.scalar_tensor_tensor(r, a, 1.0, r, ALU.add, ALU.mult).then_inc(rg_e, 1)

            def scan(k):
                dve.wait_ge(rg_x, k + 1)
                t = 2 * k + 1
                dve.wait_ge(rg_mm, min(t + 2, t // SUP * SUP + SUP))
                for t in (2 * k, 2 * k + 1):
                    m = dve.tensor_tensor_scan(xr[:, t, :], ra[:, t % 4, :], ri[:, t % 4, :], 0.0, ALU.mult, ALU.add)
                m.then_inc(rg_b, 1)

            def take_gate(j):
                b = B0["a_in"] + 10 + j
                dve.wait_ge(unit_done, U0["a_in"] + 20 + 2 * j + 2)
                dve.tensor_tensor(zb[:, j % 2, :, :], acc[:, 2 * (b % 2):2 * (b % 2) + 2, 0:TB],
                                  over2(inv[:, :]), ALU.mult).then_inc(acc_free, 1)

            def gated(j):
                dve.wait_ge(gelu_done, j + 1)
                dve.wait_ge(rg_b, j + 1)
                dve.tensor_tensor(zb[:, j % 2, :, :], zb[:, j % 2, :, :], xr[:, 2 * j:2 * j + 2, :], ALU.mult).then_inc(ry_z, 1)

            def ry_low(j):
                dve.wait_ge(ry_hi, j + 1)
                dve.tensor_tensor(rl3[:, 2 * j:2 * j + 2, :], zb[:, j % 2, :, :], rh3[:, 2 * j:2 * j + 2, :].bitcast(F32),
                                  ALU.subtract).then_inc(ry_lo, 1)

            for u in range(60):
                k = (u - 10) // 2
                if u % 2 == 0 and 0 <= k < RT // 2:
                    decay(k)
                if u >= 23 and u <= 41 and u % 2:
                    ry_low((u - 23) // 2)
                if u:
                    lo_c(U0["a_in"] + u + 2)
                if u % 2 and 0 <= (u - 11) // 2 < RT // 2:
                    scan((u - 11) // 2)
                if u < 20 and u % 2:
                    take_xr(u // 2)
                elif u < 40 and u % 2:
                    take_gate((u - 21) // 2)
                if u >= 22 and u <= 40 and u % 2 == 0:
                    gated((u - 22) // 2)
                if u >= 40 and (u - 40) % 5 == 4:
                    g = (u - 40) // 5
                    dve.wait_ge(unit_done, U0["a_in"] + u + 1)
                    for p in (0, 1):
                        t = 2 * g + p
                        h = hT[:, 2 * t:2 * t + 2, :]
                        dve.tensor_tensor(h, h, (psx if g % 2 == 0 else acc)[:, 2 * p:2 * p + 2, 0:TB], ALU.add)\
                            .then_inc(acc_free, 1)
                    for p in (0, 1):
                        g_low(2 * g + p, "g_mlp0", gh4, gl4, ALL, 24 + 2 * g + p + 1)

            def mlp(name, r, T, base, nxt, last=False):
                for c in range(4):
                    def body(i):
                        for pr in range(2):
                            for j in range(2):
                                k = U0[name] + 32 * c + 2 * pr + j
                                if not (isinstance(i, int) and pr == 0 and j == 0):
                                    lo_loop(k + 2, i, 4)
                            b = B0[name] + 16 * c + pr
                            dve.wait_ge(unit_done, i * 4 + (k + 1))
                            z = zb[:, pr, :, 0:T]
                            dve.scalar_tensor_tensor(z, acc[:, 2 * (b % 2):2 * (b % 2) + 2, 0:T], 0.0, over2(inv[:, 0:T]),
                                                     ALU.max, ALU.mult).then_inc(acc_free, 1)
                            dve.wait_ge(hid_hi, i * 2 + (base + 8 * c + pr + 1))
                            t = ds(i * 4 + 2 * pr, 2)
                            dve.tensor_tensor(fl[:, t, 0:T], z, fh[:, t, 0:T].bitcast(F32), ALU.subtract).then_inc(hid_lo, 1)
                    if c == 0:
                        root(r, T)
                        lo_c(U0[name] + 2)
                        body(0)
                    with dve.Fori(0, 3 if c == 0 else 4) as i:
                        body(i + 1 if c == 0 else i)
                    if c < 3:
                        resid_stage(name, 2, 0, None, None, None, None, nxt[-1], u_off=32 * c + 16, b_off=16 * c + 8)
                    else:
                        resid_stage(name, 2, *nxt, last=last, u_off=112, b_off=56)

            mlp("mlp0", 3, TB, NEXP, (4, "g_kv", gh5, gl5, ALL, ALL))

            def root_k():
                root(4, TB)
                lo_c(U0["v"] + 2)
                dve.wait_ge(rope_in, 16)
                for j in range(2):
                    link(dve.tensor_tensor(rq[:, j, :], rk[:, j, TOK], inv[:, TOK], ALU.mult))
                    link(dve.scalar_tensor_tensor(rk[:, j, :], rk[:, j, :], HD2 ** -0.5, inv[:, :], ALU.mult, ALU.mult))
                dve.wait_ge(lv_in, 16)
                for j in range(2):
                    link(dve.tensor_tensor(lv[:, 2 * j, :], lv[:, 2 * j, :], lv[:, 2 * j + 1, :], ALU.mult))
                    m = dve.tensor_reduce(st2[:, 12 + j:13 + j], lv[:, 2 * j, :], AX.X, ALU.add)
                    if j == 0:
                        link(m)
                m.then_inc(dl_z, 1)
                dve.memset(st2[:, 18:19], 1.0)
                dve.wait_ge(dl_exp, 1)
                link(dve.tensor_tensor(st2[:, 19:20], st2[:, 17:18], st2[:, 16:17], ALU.subtract))
                link(ts_(st2[:, 19:20], st2[:, 19:20], -LAMBDA_INIT, None, ALU.add))
                link(ts_(gsub[:, :], par("g_sub"), 1.0 - LAMBDA_INIT, None, ALU.mult))

            def rope2(t, b, to, cos, sin, tok, done):
                if t:
                    dve.wait_ge(done, t)
                elif done is q_done:
                    dve.wait_ge(k_done, DH)
                src = acc[:, 2 * (b % 2):2 * (b % 2) + 2, tok]
                T = tok.stop - tok.start
                for a, z in ((slice(0, 64), slice(64, P)), (slice(64, P), slice(0, 64))):
                    link(dve.tensor_tensor(swp[a, :, 0:T], src[z], over2(sin[z, :]), ALU.mult))
                dve.tensor_tensor(to, src, over2(cos), ALU.mult).then_inc(acc_free, 1)
                dve.wait_ge(acc_free, b + 1)
                dve.tensor_tensor(to, to, swp[:, :, 0:T], ALU.add).then_inc(done, 1)

            def take_keys2(t):
                rope2(t, B0["k"] + t, kT2[:, 2 * t:2 * t + 2, :], rk[:, 0, :], rk[:, 1, :], ALL, k_done)

            def maxima2(a):
                dve.wait_ge(a_sc, a + 1)
                dve.tensor_reduce(st2[:, 0:2], psx[:, 0, 0:2 * (META + P)].rearrange("p (c k) -> p c k", c=2), AX.X, ALU.max,
                                  negate=True)
                dve.tensor_reduce(st2[:, 2:4], psx[:, 1:3, 0:TB], AX.X, ALU.max, negate=True).then_inc(a_max, 1)

            def attn2(a):
                dve.wait_ge(a_exp, a + 1)
                c = st2[:, 8:12]
                link(dve.reciprocal(c, st2[:, 4:8]))
                tt(c.rearrange("p (i c) -> p i c", i=2), c.rearrange("p (i c) -> p i c", i=2),
                   st2[:, 18:20].unsqueeze(1).to_broadcast([P, 2, 2]), ALU.mult)
                for i, pr in enumerate((pr0, pr1)):
                    link(ts_(pr[:, 0, :], pr[:, 0, :], st2[:, 8 + 2 * i:9 + 2 * i], None, ALU.mult))
                    m = dve.scalar_tensor_tensor(pr[:, 0, :], pr[:, 1, :], st2[:, 9 + 2 * i:10 + 2 * i], pr[:, 0, :],
                                                 ALU.mult, ALU.add)
                    if i == 0:
                        link(m)
                m.then_inc(a_attn, 1)

            def take_o(a):
                dve.wait_ge(a_pv, a + 1)
                dve.tensor_copy(oT[:, 2 * a:2 * a + 2, :].rearrange("p a t -> p (a t)"), psx[:, 1, :]).then_inc(a_o, 1)

            def norm_o(a):
                dve.wait_ge(a_rt, a + 1)
                dve.wait_ge(a_o, a + 1)
                link(dve.reciprocal(ort[:, :], ort[:, :]))
                for f in range(2):
                    o = oT[:, 2 * a + f, :]
                    m = dve.scalar_tensor_tensor(o, o, gsub[:, f:f + 1], ort[:, :], ALU.mult, ALU.mult)
                    if f == 0:
                        link(m)
                m.then_inc(a_od, 1)

            def low_o(a):
                dve.wait_ge(o_hi, a + 1)
                dve.tensor_tensor(ol[:, 2 * a:2 * a + 2, :], oT[:, 2 * a:2 * a + 2, :], oh[:, 2 * a:2 * a + 2, :].bitcast(F32),
                                  ALU.subtract).then_inc(o_lo, 1)

            root_k()
            for u in range(48):
                b, t = B0["v"] + u // 2, u // 2 % 8
                a = (u - 32) // 2 - 1
                if u == 32:
                    for j in range(8):
                        g_low(j, "g_b", gh6, gl6, TOK, 40 + j + 1)
                        if j == 2:
                            take_keys2(DH - 1)
                if u >= 34 and u % 2 == 0 and a:
                    take_o(a - 1)
                if u:
                    lo_c(U0["v"] + u + 2)
                if u >= 34 and u % 2 == 0:
                    maxima2(a)
                    attn2(a)
                    if a:
                        norm_o(a - 1)
                if u % 2 and u != 31:
                    dve.wait_ge(unit_done, U0["v"] + u + 1)
                    if u < 16:
                        if t >= 2:
                            dve.wait_ge(v_mm, t - 1)
                        dve.tensor_tensor(zb[:, t % 2, :, :], acc[:, 2 * (b % 2):2 * (b % 2) + 2, 0:TB],
                                          over2(inv[:, :]), ALU.mult).then_inc(acc_free, 1)
                    elif u < 32:
                        take_keys2(t)
                    else:
                        if t >= 2:
                            dve.wait_ge(a_sc, t - 1)
                        rope2(t, b, q2[:, t % 2, :, :], rq[:, 0, :], rq[:, 1, :], QT, q_done)
            for a in range(DH - 2):
                low_o(a)
                if a == 1:
                    take_o(DH - 2)
            for j in range(4):
                lo_c(U0["o"] + j + 2)
                if j == 0:
                    maxima2(DH - 1)
                    attn2(DH - 1)
                    norm_o(DH - 2)
                    low_o(DH - 2)
                elif j == 1:
                    take_o(DH - 1)
                    norm_o(DH - 1)
                    low_o(DH - 1)
                else:
                    t = j - 2
                    b = B0["o"] + t
                    dve.wait_ge(unit_done, U0["o"] + j + 1)
                    h = hT[:, 2 * t:2 * t + 2, TOK]
                    dve.tensor_tensor(h, h, acc[:, 2 * (b % 2):2 * (b % 2) + 2, 0:S], ALU.add).then_inc(acc_free, 1)
            for t in range(2):
                g_low(t, "g_mlp1", gh7, gl7, TOK, 48 + t + 1)

            def body(i):
                for pr in range(2):
                    for j in range(2):
                        k = U0["o"] + 4 + 2 * pr + j
                        lo_loop(k + 2, i, 4)
                    b = B0["o"] + 2 + pr
                    dve.wait_ge(unit_done, i * 4 + (k + 1))
                    h = hT[:, ds(i * 4 + (4 + 2 * pr), 2), TOK]
                    dve.tensor_tensor(h, h, acc[:, 2 * (b % 2):2 * (b % 2) + 2, 0:S], ALU.add).then_inc(acc_free, 1)
                    g_low(i * 2 + (2 + pr), "g_mlp1", gh7, gl7, TOK, i * 2 + (48 + 2 + pr + 1))
            with dve.Fori(0, 3) as i:
                body(i)
            mlp("mlp1", 5, S, NEXP + 32, (7, None, None, None, TOK, TOK), last=True)
            root(6, S)
            for j in range(4):
                for kt in range(4 * j, 4 * j + 4):
                    m = dve.scalar_tensor_tensor(result[:, kt, :], hT[:, kt, TOK], col("g_final", kt), inv[:, 0:S],
                                                 ALU.mult, ALU.mult)
                m.then_inc(result_ready, 1)

        @block.gpsimd
        def _(pool):
            chain = Chain(pool, chain_pool)
            link = chain.link

            def over2(ap):
                return ap.unsqueeze(1).to_broadcast([ap.shape[0], 2, ap.shape[-1]])

            pool.wait_ge(x_in[3], 16)
            pool.dma_start(hT[:, :, 0:META], A["meta"].rearrange("(kt p) t -> p kt t", p=P)).then_inc(meta_in, 16)

            def rope(m, to):
                pool.wait_ge(head_n, m + 1)
                if m == 0:
                    pool.wait_ge(table_ready, 1)
                if m == 5:
                    pool.wait_ge(raw_aux, 4)
                link(pool.tensor_tensor(to, xn[:, :, :], over2(ropec[:, :]), ALU.mult))
                pool.wait_ge(head_s, m + 1)
                pool.tensor_tensor(to, to, xs[:, :, :], ALU.add).then_inc(head_done, 1)

            for m in range(4):
                rope(m, qT[:, 2 * m:2 * m + 2, :])
                if m == 0:
                    pool.wait_ge(x_summed, 1)
                    pool.wait_ge(table_ready, 1)
                    for j, n in enumerate(("cmp_w1_k", "cmp_w1_v")):
                        pool.dma_start(cw1[j][:, :, :], A[n].rearrange("(kt p) n -> p kt n", p=P)).then_inc(cw_in, 16)
            rope(4, krope[:, :, :])
            rope(5, krope[:, :, :])

            def windows(n):
                g = POOL_ORDER[n]
                pool.wait_ge(acc_free, B0["pool"] + n + 1)
                if n == 0:
                    pool.wait_ge(chid_mm, 1)
                u = a = xp[:, n % 2, :, :]
                for k in range(g + 1):
                    sh = 1 << k
                    b = pw[:, 1 + k % 2, :, :]
                    pool.tensor_copy(b[:, :, 0:sh], a[:, :, 0:sh])
                    link(pool.tensor_tensor(b[:, :, sh:S], a[:, :, sh:S], a[:, :, 0:S - sh], ALU.add))
                    a = b
                W = 2 << g
                b = pw[:, 0, :, :]
                if n:
                    pool.wait_ge(pooled_lo, n)
                pool.tensor_scalar(b[:, :, W:S], a[:, :, W:S], 1.0 / W, None, ALU.mult)
                link(pool.tensor_tensor(b[:, :, 0:W], a[:, :, 0:W], over2(par("rcnt", 0, W)), ALU.mult))
                pool.tensor_tensor(b, b, u, ALU.subtract).then_inc(pooled, 1)

            for g in range(4):
                windows(g)
            pool.wait_ge(pooled_lo, 4)
            pool.dma_start(wh[:, :, :], A["w_head_out"].rearrange("h d e -> d h e")).then_inc(wh_in, 16)

            def sum_squares(r, T):
                pool.wait_ge(stat_mm, r)
                m = pool.memset(sqsum[:, 0:T], 0.0)
                if r == 1:
                    m.then_inc(sq_used, 2)
                else:
                    link(m)
                with pool.Fori(0, 4) as i:
                    for pr in range(2):
                        pool.wait_ge(sq_ready, i * 2 + (8 * (r - 1) + pr + 1))
                        pool.wait_ge(sq_used, i * 2 + (8 * (r - 1) + pr + 2))
                        pool.tensor_tensor(sq[:, pr, 0, 0:T], sq[:, pr, 0, 0:T], sq[:, pr, 1, 0:T], ALU.add).then_inc(sq_half, 1)
                        pool.wait_ge(sq_half, i * 2 + (8 * (r - 1) + pr + 1))
                        pool.tensor_tensor(sqsum[:, 0:T], sqsum[:, 0:T], sq[:, pr, 0, 0:T], ALU.add).then_inc(sq_used, 1)

            pool.wait_ge(y_done, NKV)
            pool.tensor_tensor(rg[:, :, :], par("router").rearrange("p (kt n) -> p kt n", n=20),
                               par("g_ffn").unsqueeze(2).to_broadcast([P, KT, 20]), ALU.mult).then_inc(rg_ready, 1)
            sum_squares(1, S)
            sum_squares(2, TB)
            pool.wait_ge(unit_done, U0["a_in"])
            pool.memset(band[:, :, :], 0.0).then_inc(band_clear, 1)
            for k in range(RT // 2):
                q = slice(2 * (k % 2), 2 * (k % 2) + 2)
                pool.wait_ge(rg_sig, 2 * k + 2)
                pool.tensor_tensor(ri[:, q, :], ri[:, q, :], xr[:, 2 * k:2 * k + 2, :], ALU.mult).then_inc(rg_i, 1)
                pool.wait_ge(rg_i, k + 1)
                pool.wait_ge(rg_e, k + 1)
                pool.tensor_tensor(ri[:, q, :], ri[:, q, :], rr[:, q, :], ALU.mult).then_inc(rg_x, 1)
            sum_squares(3, TB)
            pool.dma_start(rk[:, :, :], A["rope2"].rearrange("p (a t) -> p a t", a=2)).then_inc(rope_in, 16)
            pool.dma_start(lv[:, :, :].rearrange("p a d -> p (a d)"), A["lam_vecs"].to_broadcast([P, 4 * HD2]))\
                .then_inc(lv_in, 16)
            sum_squares(4, TB)
            sum_squares(5, S)
            sum_squares(6, S)


def _packed(inputs):
    i = {k: np.asarray(v) for k, v in inputs.items()}

    def tiles(a):
        return np.ascontiguousarray(a.reshape(-1, P).T)

    cols = [a.astype(np.float32) for _, a in const_parts()]
    cols += [tiles(i[n].reshape(-1)) for n in ("attn_norm_g", "ffn_norm_g", "a_norm_g_2")]
    cols += [tiles(i["mlp_norm_g_2"][0]), tiles(i["kv_norm_g_2"]), tiles(i["b_norm_g_2"][0]),
             tiles(i["mlp_norm_g_2"][1]), tiles(i["final_norm_g_2"]), tiles(i["pool_scale"][0])]
    cols += [tiles(i["a_conv_w_2"][0]), tiles(i["a_conv_b_2"][0]), tiles(i["a_b_r_2"][0]),
             tiles(i["a_b_i_2"][0]), tiles(i["a_lambda_2"][0])]
    cols += [np.tile(i[n][0][:, None], (2, 1)) for n in ("q_norm_g", "k_norm_cmp_g", "k_norm_slc_g", "k_norm_swa_g")]
    cols += [tiles(i["b_subln_g_2"][0])]
    cols += [i[n][0].reshape(16, 2, HD).transpose(1, 2, 0).reshape(P, 16) for n in ("cmp_pos_emb_k", "cmp_pos_emb_v")]
    w2k = i["cmp_w2_k"][0].reshape(2, P, HD).transpose(1, 0, 2)
    cols += [np.concatenate([w2k, w2k], axis=2).reshape(P, 2 * P),
             i["cmp_w2_v"][0].reshape(2, P, HD).transpose(1, 0, 2).reshape(P, 2 * HD)]
    router = np.concatenate([i["w_router_group"][0], i["w_router_expert"][0]], axis=1)
    cols += [router.reshape(KT, P, 20).transpose(1, 0, 2).reshape(P, KT * 20)]
    cols += [np.tile(np.concatenate([i["b_router_group"][0], i["b_router_expert"][0]])[None, :], (P, 1))]
    return np.ascontiguousarray(np.concatenate(cols, axis=1))


def arrays_of(inputs):
    i = {k: np.asarray(v) for k, v in inputs.items()}
    masks = np.concatenate([a for _, a in mask_parts()], axis=1).astype(np.float32)
    a = {
        "x": np.ascontiguousarray(i["x"][0].T), "meta": np.ascontiguousarray(i["meta_tokens_2"].T),
        "aux": _packed(i), "mask": masks, "positions": i["positions"],
        "w_in": i["w_in"][0], "cmp_w1_k": i["cmp_w1_k"][0], "cmp_w1_v": i["cmp_w1_v"][0],
        "w_head_out": i["w_head_out"][0], "w_pool": i["w_pool"][0], "w_out": i["w_out"][0],
        "rope2": np.concatenate([x for _, x in rope2_parts()], axis=1).astype(np.float32),
        "w_expert_gate": i["w_expert_gate"][0], "w_expert_up": i["w_expert_up"][0],
        "w_expert_down": i["w_expert_down"][0].reshape(NEXP * DEXP, D),
        "a_w_in": i["a_w_in_2"][0], "a_w_ri": np.stack([i["a_w_r_2"][0], i["a_w_i_2"][0]]), "a_w_out": i["a_w_out_2"][0],
        "w_kv": i["w_kv_2"], "w_q": i["b_w_q_2"][0], "lam_vecs": i["b_lambda_2"][0].reshape(1, 4 * HD2),
        "w_o": i["b_w_o_2"][0],
        "mlp_w1": i["mlp_w1_2"].reshape(2 * D, D_FF), "mlp_w2": i["mlp_w2_2"].reshape(2 * D_FF, D),
    }
    return {k: np.ascontiguousarray(v) for k, v in a.items()}


def kernel(**inputs):
    from concourse import bacc
    from concourse.bass_utils import run_bass_kernel_spmd

    nc = bacc.Bacc("TRN2", target_bir_lowering=False, num_devices=1)
    arrays = arrays_of(inputs)
    A = {k: nc.dram_tensor(f"in_{k}", v.shape, mybir.dt.from_np(v.dtype), kind="ExternalInput").ap()
         for k, v in arrays.items()}
    out = nc.dram_tensor("out", [D, S], F32, kind="ExternalOutput").ap()
    mixer_moe_rnn_attention(nc, A, out)
    r = run_bass_kernel_spmd(nc, [{f"in_{k}": v for k, v in arrays.items()}], core_ids=[0])
    return np.ascontiguousarray(r.results[0]["out"].T)[None]
```
